# Optimizing a Trainium2 kernel written in Bass

```python
import math
import jax, jax.numpy as jnp
from jax import lax
import numpy as np

D_MODEL = 1024
BATCH = 1
SEQ = 512
DEPTH = 1

POOL_WIDTH = 512
POOL_WINDOWS = (2, 4, 8, 16)
POOL_GROUPS = 4
POOL_GROUP_DIM = POOL_WIDTH // POOL_GROUPS
SGU_WIDTH = 512
SGU_CHUNK = 128
SGU_HEADS = 4
SGU_HEAD_DIM = SGU_WIDTH // SGU_HEADS
SSM_WIDTH = 512
SSM_GROUP_DIM = 16
SSM_GROUPS = SSM_WIDTH // SSM_GROUP_DIM
SSM_STATE = 64
N_BRANCHES = 3
BRANCH_WIDTH = 512
IN_COLS = POOL_WIDTH + 2 * SGU_WIDTH + SSM_WIDTH + N_BRANCHES * D_MODEL
N_GROUPS = 4
EXPERTS_PER_GROUP = 8
N_EXPERTS = N_GROUPS * EXPERTS_PER_GROUP
EXPERT_TOP_K = 2
D_EXPERT = D_MODEL // 2
EPS = 1e-6

kernel_name = "hybrid_pool_sgu_s5_hmoe"

F32 = jnp.float32

def rmsnorm(x, g):
    xf = x.astype(F32)
    y = xf * lax.rsqrt(jnp.mean(xf * xf, axis=-1, keepdims=True) + EPS)
    return (y * g.astype(F32)).astype(x.dtype)

def layernorm(x, g, b):
    xf = x.astype(F32)
    mu = jnp.mean(xf, axis=-1, keepdims=True)
    var = jnp.mean(jnp.square(xf - mu), axis=-1, keepdims=True)
    y = (xf - mu) * lax.rsqrt(var + EPS)
    return (y * g.astype(F32) + b.astype(F32)).astype(x.dtype)

def pool_mixer(xa, pool_w, pool_scale):
    B_, L, _ = xa.shape
    xf = xa.astype(F32)
    maxw = POOL_WINDOWS[-1]
    cs = jnp.cumsum(xf, axis=1)
    cp = jnp.pad(cs, ((0, 0), (maxw + 1, 0), (0, 0)))
    pos = jnp.arange(L)
    outs = []
    for gi, w in enumerate(POOL_WINDOWS):
        ch = slice(gi * POOL_GROUP_DIM, (gi + 1) * POOL_GROUP_DIM)
        count = jnp.minimum(pos + 1, w).astype(F32)[:, None]
        win_sum = cp[:, maxw + 1:maxw + 1 + L, ch] - cp[:, maxw + 1 - w:maxw + 1 - w + L, ch]
        outs.append(win_sum / count - xf[..., ch])
    diff = jnp.stack(outs, axis=2)
    y = jnp.einsum('blgc,gcd->blgd', diff, pool_w.astype(F32)).reshape(B_, L, POOL_WIDTH)
    return (y * pool_scale.astype(F32)).astype(xa.dtype)

def sgu_mixer(xb, ln_g, ln_b, w_s, b_s):
    z = jax.nn.gelu(xb)
    u, v = jnp.split(z, 2, axis=-1)
    v = layernorm(v, ln_g, ln_b)
    B_, L, _ = v.shape
    n_chunks = L // SGU_CHUNK
    v = v.reshape(B_, n_chunks, SGU_CHUNK, SGU_HEADS, SGU_HEAD_DIM)
    mask = jnp.tril(jnp.ones((SGU_CHUNK, SGU_CHUNK), dtype=bool))[None]
    w = jnp.where(mask, w_s, jnp.zeros_like(w_s))
    s = jnp.einsum('hts,bnshc->bnthc', w, v) + b_s.T[None, None, :, :, None]
    return u * s.reshape(B_, L, SGU_WIDTH)

def _ssm_combine(e1, e2):
    a1, b1 = e1
    a2, b2 = e2
    return a1 * a2, a2 * b1 + b2

def s5_mixer(xc, a_re, a_im, log_dt, b_re, b_im, c_re, c_im, d_skip, glu_w, glu_b):
    B_, L, _ = xc.shape
    lam = lax.complex(a_re.astype(F32), a_im.astype(F32))
    dt = jnp.exp(log_dt.astype(F32))[:, None]
    lam_bar = jnp.exp(lam * dt)
    b = lax.complex(b_re.astype(F32), b_im.astype(F32))
    b_bar = ((lam_bar - 1.0) / lam)[..., None] * b
    c = lax.complex(c_re.astype(F32), c_im.astype(F32))
    u = xc.astype(F32).reshape(B_, L, SSM_GROUPS, SSM_GROUP_DIM)
    bu = jnp.einsum('blgc,gpc->blgp', u.astype(jnp.complex64), b_bar)
    a = jnp.broadcast_to(lam_bar, bu.shape)
    _, states = lax.associative_scan(_ssm_combine, (a, bu), axis=1)
    y = jnp.einsum('blgp,gcp->blgc', states, c).real
    y = y + d_skip.astype(F32).reshape(SSM_GROUPS, SSM_GROUP_DIM) * u
    y = jax.nn.gelu(y.reshape(B_, L, SSM_WIDTH))
    y = y * jax.nn.sigmoid(y @ glu_w.astype(F32) + glu_b.astype(F32))
    return y.astype(xc.dtype)

def hier_moe(h, rg_w, rg_b, re_w, re_b, w_gate, w_up, w_down):
    B_, L, D = h.shape
    t = h.reshape(-1, D)
    g_logits = (t @ rg_w + rg_b).astype(F32)
    g_probs = jax.nn.softmax(g_logits, axis=-1)
    g_val, g_idx = lax.top_k(g_probs, 1)
    e_logits = (t @ re_w + re_b).astype(F32).reshape(-1, N_GROUPS, EXPERTS_PER_GROUP)
    e_sel = jnp.take_along_axis(e_logits, g_idx[:, :, None], axis=1)[:, 0]
    e_val, e_idx = lax.top_k(e_sel, EXPERT_TOP_K)
    e_w = jax.nn.softmax(e_val, axis=-1) * g_val
    global_idx = g_idx * EXPERTS_PER_GROUP + e_idx
    combine = jnp.einsum('tk,tke->te', e_w,
                         jax.nn.one_hot(global_idx, N_EXPERTS, dtype=F32)).astype(h.dtype)
    out = jnp.zeros_like(t)
    for e in range(N_EXPERTS):
        y = (jax.nn.silu(t @ w_gate[e]) * (t @ w_up[e])) @ w_down[e]
        out = out + combine[:, e:e + 1] * y
    return out.reshape(B_, L, D)

def setup_inputs(seed: int = 0) -> dict:
    key = jax.random.key(seed)
    ks = jax.random.split(key, 32)
    nrm = jax.random.normal
    D = D_MODEL
    G, P, C = SSM_GROUPS, SSM_STATE, SSM_GROUP_DIM
    x = nrm(ks[0], (BATCH, SEQ, D), F32)
    norm_mix_g = 1.0 + 0.02 * nrm(ks[1], (DEPTH, D), F32)
    w_in = nrm(ks[2], (DEPTH, D, IN_COLS), F32) * D ** -0.5
    b_gate = 0.02 * nrm(ks[3], (DEPTH, N_BRANCHES * D), F32)
    pool_w = nrm(ks[4], (DEPTH, POOL_GROUPS, POOL_GROUP_DIM, POOL_GROUP_DIM), F32) * POOL_GROUP_DIM ** -0.5
    pool_scale = 1.0 + 0.02 * nrm(ks[5], (DEPTH, POOL_WIDTH), F32)
    sgu_ln_g = 1.0 + 0.02 * nrm(ks[6], (DEPTH, SGU_WIDTH), F32)
    sgu_ln_b = 0.02 * nrm(ks[7], (DEPTH, SGU_WIDTH), F32)
    sgu_w = 0.5 * nrm(ks[8], (DEPTH, SGU_HEADS, SGU_CHUNK, SGU_CHUNK), F32) * SGU_CHUNK ** -0.5
    sgu_b = 1.0 + 0.02 * nrm(ks[9], (DEPTH, SGU_HEADS, SGU_CHUNK), F32)
    ssm_a_re = -0.5 + 0.01 * nrm(ks[10], (DEPTH, G, P), F32)
    ssm_a_im = math.pi * jnp.arange(P, dtype=F32)[None, None, :] + 0.01 * nrm(ks[11], (DEPTH, G, P), F32)
    ssm_log_dt = jax.random.uniform(ks[12], (DEPTH, G), F32, math.log(1e-3), math.log(1e-1))
    ssm_b_re = nrm(ks[13], (DEPTH, G, P, C), F32) * (0.5 / C) ** 0.5
    ssm_b_im = nrm(ks[14], (DEPTH, G, P, C), F32) * (0.5 / C) ** 0.5
    ssm_c_re = nrm(ks[15], (DEPTH, G, C, P), F32) * (0.5 / P) ** 0.5
    ssm_c_im = nrm(ks[16], (DEPTH, G, C, P), F32) * (0.5 / P) ** 0.5
    ssm_d = nrm(ks[17], (DEPTH, SSM_WIDTH), F32)
    glu_w = nrm(ks[18], (DEPTH, SSM_WIDTH, SSM_WIDTH), F32) * SSM_WIDTH ** -0.5
    glu_b = 0.02 * nrm(ks[19], (DEPTH, SSM_WIDTH), F32)
    w_branch = nrm(ks[20], (DEPTH, N_BRANCHES, BRANCH_WIDTH, D), F32) * BRANCH_WIDTH ** -0.5
    w_out = nrm(ks[21], (DEPTH, D, D), F32) * D ** -0.5
    norm_ffn_g = 1.0 + 0.02 * nrm(ks[22], (DEPTH, D), F32)
    router_group_w = nrm(ks[23], (DEPTH, D, N_GROUPS), F32) * D ** -0.5
    router_group_b = 0.01 * nrm(ks[24], (DEPTH, N_GROUPS), F32)
    router_expert_w = nrm(ks[25], (DEPTH, D, N_EXPERTS), F32) * D ** -0.5
    router_expert_b = 0.01 * nrm(ks[26], (DEPTH, N_EXPERTS), F32)
    exp_w_gate = nrm(ks[27], (DEPTH, N_EXPERTS, D, D_EXPERT), F32) * D ** -0.5
    exp_w_up = nrm(ks[28], (DEPTH, N_EXPERTS, D, D_EXPERT), F32) * D ** -0.5
    exp_w_down = nrm(ks[29], (DEPTH, N_EXPERTS, D_EXPERT, D), F32) * D_EXPERT ** -0.5
    norm_final_g = 1.0 + 0.02 * nrm(ks[30], (D,), F32)
    return {"x": x, "norm_mix_g": norm_mix_g, "w_in": w_in, "b_gate": b_gate,
            "pool_w": pool_w, "pool_scale": pool_scale,
            "sgu_ln_g": sgu_ln_g, "sgu_ln_b": sgu_ln_b, "sgu_w": sgu_w, "sgu_b": sgu_b,
            "ssm_a_re": ssm_a_re, "ssm_a_im": ssm_a_im, "ssm_log_dt": ssm_log_dt,
            "ssm_b_re": ssm_b_re, "ssm_b_im": ssm_b_im, "ssm_c_re": ssm_c_re, "ssm_c_im": ssm_c_im,
            "ssm_d": ssm_d, "glu_w": glu_w, "glu_b": glu_b,
            "w_branch": w_branch, "w_out": w_out, "norm_ffn_g": norm_ffn_g,
            "router_group_w": router_group_w, "router_group_b": router_group_b,
            "router_expert_w": router_expert_w, "router_expert_b": router_expert_b,
            "exp_w_gate": exp_w_gate, "exp_w_up": exp_w_up, "exp_w_down": exp_w_down,
            "norm_final_g": norm_final_g}

def reference(x, norm_mix_g, w_in, b_gate, pool_w, pool_scale, sgu_ln_g, sgu_ln_b, sgu_w, sgu_b,
              ssm_a_re, ssm_a_im, ssm_log_dt, ssm_b_re, ssm_b_im, ssm_c_re, ssm_c_im, ssm_d,
              glu_w, glu_b, w_branch, w_out, norm_ffn_g, router_group_w, router_group_b,
              router_expert_w, router_expert_b, exp_w_gate, exp_w_up, exp_w_down, norm_final_g):
    B_, L, D = x.shape
    a_end = POOL_WIDTH
    b_end = a_end + 2 * SGU_WIDTH
    c_end = b_end + SSM_WIDTH
    for l in range(DEPTH):
        h = rmsnorm(x, norm_mix_g[l])
        proj = h @ w_in[l]
        ya = pool_mixer(proj[..., :a_end], pool_w[l], pool_scale[l])
        yb = sgu_mixer(proj[..., a_end:b_end], sgu_ln_g[l], sgu_ln_b[l], sgu_w[l], sgu_b[l])
        yc = s5_mixer(proj[..., b_end:c_end], ssm_a_re[l], ssm_a_im[l], ssm_log_dt[l],
                      ssm_b_re[l], ssm_b_im[l], ssm_c_re[l], ssm_c_im[l], ssm_d[l],
                      glu_w[l], glu_b[l])
        ys = jnp.stack([ya, yb, yc], axis=2)
        branches = jnp.einsum('blkc,kcd->blkd', ys, w_branch[l])
        gates = jax.nn.sigmoid(proj[..., c_end:].reshape(B_, L, N_BRANCHES, D)
                               + b_gate[l].reshape(N_BRANCHES, D))
        merged = jnp.sum(gates * branches, axis=2)
        x = x + merged @ w_out[l]
        h2 = rmsnorm(x, norm_ffn_g[l])
        x = x + hier_moe(h2, router_group_w[l], router_group_b[l], router_expert_w[l],
                         router_expert_b[l], exp_w_gate[l], exp_w_up[l], exp_w_down[l])
    return rmsnorm(x, norm_final_g)


_drawn_inputs = setup_inputs


def setup_inputs(seed=0):
    import zlib

    import numpy as np

    out = dict(_drawn_inputs(seed))
    spreads = {}
    factors = {'b_gate': 4.864,
     'pool_scale': 10.935,
     'sgu_ln_g': 42.133,
     'sgu_ln_b': 45.098,
     'sgu_b': 17.909,
     'ssm_a_re': 64.0,
     'ssm_a_im': 25.816,
     'ssm_log_dt': 22.056,
     'ssm_b_re': 28.352,
     'ssm_b_im': 34.88,
     'ssm_c_re': 29.752,
     'ssm_c_im': 46.248,
     'glu_b': 54.973,
     'router_group_b': 33.712,
     'router_expert_b': 18.471,
     'norm_final_g': 21.139,
     'norm_ffn_g': 4.989,
     'glu_w': 5.353}
    for name, (base, spread) in spreads.items():
        noise = np.random.default_rng([zlib.crc32(name.encode()), seed]).standard_normal(out[name].shape)
        drawn = base * np.exp(spread * noise) if base else spread * noise
        out[name] = __import__('jax').numpy.asarray(drawn.astype(out[name].dtype))
    for name, factor in factors.items():
        out[name] = (out[name] * factor).astype(out[name].dtype)
    return out
```

```python
from contextlib import ExitStack
import math

import numpy as np
import concourse.bass as bass
from concourse import mybir

F32 = mybir.dt.float32
I32 = mybir.dt.int32
U32 = mybir.dt.uint32
ALU = mybir.AluOpType
ACT = mybir.ActivationFunctionType
X = mybir.AxisListType.X

P = 128
T = 512
NT = T // P
D = 1024
KD = D // P
W = 512
MW = W // P
EPS = 1e-6

G = 32
Q = G // 2
S = 64
CH = 16
J = 8
NC = T // J

NE = 32
F = 512
KF = F // P
CAP = 64
NOV = 2 * T // CAP - 1
NB = NE + NOV
BIG = 3.0e38
MAGIC = 12582912.0

C_SSM, C_V, C_POOL, C_U = 1536, 1024, 0, 512
GATE_STEPS = [(half, k) for half in range(2) for k in range(3)]
WIN_COLS = [C_SSM, C_V, C_POOL, C_U] + [2048 + k * D + half * W for half, k in GATE_STEPS]

PRM = ["are", "aim", "ldt", "dt", "r", "th", "n", "n2", "t1", "t2", "t3", "thr", "nhalf", "s", "c", "cosm1",
       "cos", "sin", "e1", "rho", "tanh", "one_m", "inv", "em1", "nr", "ni", "m2", "wr", "wi",
       "cr1", "ci1", "cr2", "ci2", "ab"]



def psum_groups():
    g = ["par", "ct", "wst"]
    g += [("x", i, h) for i in range(NT) for h in range(2)]
    g += [("c", m) for m in range(MW)] + [("v", i) for i in range(NT)]
    g += [("bt", r, i) for r in range(2) for i in range(4)] + [("k", i) for i in range(8)]
    g += [("a", m) for m in range(MW)] + [("bu", h, r) for h in range(2) for r in range(2)]
    g += [("u", m) for m in range(MW)] + [("py", m) for m in range(MW)] + [("sg", h) for h in range(4)]
    g += [("y", i) for i in range(4)]
    for n in range(len(GATE_STEPS)):
        g += [f for m in range(MW) for f in (("gt", n, m), ("br", n, m))]
        if n == 1:
            g += [("gl", m) for m in range(MW)]
    for i in range(NT):
        g += [("o", i, 0), ("o", i, 1)]
        if i >= 1:
            g += [("rt", i - 1, 0), ("rt", i - 1, 1), ("lg", i - 1)]
    g += [("rt", NT - 1, 0), ("rt", NT - 1, 1), ("lg", NT - 1), "pos", "tok"]
    return {name: (i % 8, i // 8 + 1) for i, name in enumerate(g)}


class Steps:

    def __init__(self, eng, sem):
        self.eng, self.sem, self.n = eng, sem, 0

    def mark(self, ins):
        self.n += 1
        ins.then_inc(self.sem, 1)

    def wait(self):
        self.eng.wait_ge(self.sem, self.n)

    def then(self, ins):
        self.mark(ins)
        self.wait()


def trunk(nc, x, norm_mix_g, w_in, b_gate, pool_w, pool_scale, sgu_ln_g, sgu_ln_b, sgu_w, sgu_b,
          ssm_a_re, ssm_a_im, ssm_log_dt, ssm_b_re, ssm_b_im, ssm_c_re, ssm_c_im, ssm_d, glu_w, glu_b,
          w_branch, w_out, norm_ffn_g, router_group_w, router_group_b, router_expert_w, router_expert_b,
          exp_w_gate, exp_w_up, exp_w_down, norm_final_g, out):
    place = psum_groups()

    xc_d = nc.dram_tensor("xc_scratch", (W, T), F32, kind="Internal").ap()
    y_d = nc.dram_tensor("y_scratch", (W, T), F32, kind="Internal").ap()
    h2_d = nc.dram_tensor("h2_scratch", (T, D), F32, kind="Internal").ap()
    tok_d = nc.dram_tensor("token_of_slot", (NB * CAP, 1), F32, kind="Internal").ap()
    res_d = nc.dram_tensor("result_rows", (NB * CAP, D), F32, kind="Internal").ap()

    with ExitStack() as ctx:
        ctx.enter_context(nc.allow_non_contiguous_dma(reason="small parameter vectors"))

        def sb(name, shape, dt=F32):
            return ctx.enter_context(nc.sbuf_tensor(name, shape, dt))

        def sem(name):
            return ctx.enter_context(nc.semaphore(name))

        ps = ctx.enter_context(nc.psum_tensor("ps", [P, 8, 512], F32))

        ring = sb("ring", [P, 6, 4096])
        xb = sb("xb", [P, 4096])
        hb = sb("hb", [P, 4096])
        ab = sb("ab", [P, 2048])
        ub = sb("ub", [P, 2048])
        cb = sb("cb", [P, 2048])
        vb = sb("vb", [P, 2048])
        mb = sb("mb", [P, 4096])
        ident = sb("ident", [P, P])
        lng = sb("lng", [P, W])
        lnb = sb("lnb", [P, W])
        wst = sb("wst", [P, 4, P])
        poolw = sb("poolw", [P, 4, P])
        prm = sb("prm", [P, len(PRM), Q])
        pw_re = sb("pw_re", [P, J + 1, Q])
        pw_im = sb("pw_im", [P, J + 1, Q])
        pwrev = sb("pwrev", [P, 2, J, Q])
        icnt = sb("icnt", [P, 16])
        cols = sb("cols", [P, 64])
        stat = sb("stat", [P, 64])
        mean_var = sb("mean_var", [P, 2 * NT])
        bs_row = sb("bs_row", [1, 4, P])
        ones_row = sb("ones_row", [1, P])
        rbias = sb("rbias", [1, 36])
        iot_i = sb("iot_i", [P, 52], I32)
        iot = sb("iot", [P, 52])
        zeros = sb("zeros", [NB, CAP])
        idx_u = sb("idx_u", [CAP, NB], U32)
        idx_now = sb("idx_now", [CAP, 3], U32)
        row_u = sb("row_u", [P, 8], U32)
        wts = sb("wts", [P, 8])
        ovi = sb("ovi", [1, 16], I32)

        BG, GB, PSC, DSK, GMX, GFF, GFX = 0, 24, 28, 32, 36, 44, 52
        x3 = xb[:].rearrange("p (i d) -> p i d", i=NT)
        toep = xb[:].rearrange("p (g n) -> p g n", g=G)
        hT = hb[:].rearrange("p (k t) -> p k t", k=KD)
        A = ab[:].rearrange("p (m t) -> p m t", m=MW)
        U = ub[:].rearrange("p (m t) -> p m t", m=MW)
        C = cb[:].rearrange("p (m t) -> p m t", m=MW)
        V = vb[:].rearrange("p (m t) -> p m t", m=MW)
        M = mb[:].rearrange("p (k t) -> p k t", k=KD)
        slot_k = [ring[:, s].rearrange("p (k n) -> p k n", k=KD) for s in range(6)]
        slot_h = [ring[:, s].rearrange("p (k n) -> p k n", k=KF) for s in range(6)]

        spare = ring[:, 2:5].rearrange("p s n -> p (s n)")
        NCP = Q * (J + 1) * CH
        cp_re = spare[:, 0:NCP].rearrange("p (q j c) -> p q j c", q=Q, j=J + 1)
        cp_im = spare[:, NCP:2 * NCP].rearrange("p (q j c) -> p q j c", q=Q, j=J + 1)
        o = 2 * NCP
        u8 = spare[:, o:o + 2048]
        y8 = spare[:, o + 2048:o + 4096]
        st = spare[:, o + 4096:o + 6144]
        tmp6 = spare[:, o + 6144:o + 7680]
        assert o + 7680 == 3 * 4096
        ctmp = spare[:, o + 2048:o + 2048 + NCP]
        btT = [ring[:, 5, Q * P * r:Q * P * (r + 1)].rearrange("p (q n) -> p q n", q=Q) for r in range(2)]
        u8v = u8.rearrange("p (g c) -> p g c", g=G)
        y8v = y8.rearrange("p (g c) -> p g c", g=G)
        yT = u8.rearrange("p (m t) -> p m t", m=MW)
        st_re = st[:, 0:Q * NC].rearrange("p (q c) -> p q c", q=Q)
        st_im = st[:, Q * NC:2 * Q * NC].rearrange("p (q c) -> p q c", q=Q)
        tab_c = y8[:, 0:Q * NC].rearrange("p (q c) -> p q c", q=Q)
        tab_s = y8[:, Q * NC:2 * Q * NC].rearrange("p (q c) -> p q c", q=Q)
        rot = [tmp6[:, 512 * i:512 * (i + 1)].rearrange("p (q c) -> p q c", q=Q // 2) for i in range(3)]
        PAD = 16
        win = [tmp6[:, (PAD + T) * i:(PAD + T) * (i + 1)] for i in range(2)]
        bt_pre = [mb[:, Q * P * r:Q * P * (r + 1)].rearrange("p (q j c) -> p q j c", q=Q, j=J) for r in range(2)]
        ker = mb[0:CH].rearrange("p (g n) -> p g n", g=G)
        gluw = mb[:, 2048:4096].rearrange("p (k n) -> p k n", k=MW)
        b_raw = [ub[:, 256 * r:256 * (r + 1)].rearrange("p (q c) -> p q c", q=Q) for r in range(2)]
        b_bar = [ub[:, 512 + 256 * r:768 + 256 * r].rearrange("p (q c) -> p q c", q=Q) for r in range(2)]
        c_T = [ub[:, 1024 + 256 * r:1280 + 256 * r].rearrange("p (q c) -> p q c", q=Q) for r in range(2)]
        c_nat = [ub[:, 1536 + 256 * r:1792 + 256 * r].rearrange("p (t n) -> p t n", t=2) for r in range(2)]
        sgw_nat = vb[:, 0:512].rearrange("p (h s) -> p h s", h=4)
        par_nat = vb[0:Q, 512:512 + 3 * P].rearrange("q (n p) -> q n p", n=3)
        ldt_nat = vb[0:Q, 1024:1026]

        wb_slot = [ring[:, 5, 2048 * i:2048 * (i + 1)].rearrange("p (k n) -> p k n", k=MW) for i in range(2)]
        rw = vb[:, 0:KD * 36].rearrange("p (k n) -> p k n", k=KD)
        sig = [vb[:, 512 + 512 * i:1024 + 512 * i] for i in range(2)]
        prod = vb[:, 1536:2048]
        h2n = [hb[:, 1024 * i:1024 * (i + 1)] for i in range(2)]
        h2T = hb[:, 2048:3072].rearrange("p (k t) -> p k t", k=KD)
        tok_rows = hb[0:NB, 4032:4096]

        xg = [ab[0:CAP, 1024 * b:1024 * (b + 1)] for b in range(2)]
        xgT = [ub[:, 512 * b:512 * (b + 1)].rearrange("p (k t) -> p k t", k=KD) for b in range(2)]
        silu = [ub[:, 1024 + 256 * b:1280 + 256 * b] for b in range(2)]
        act_ = [ub[:, 1536 + 256 * b:1792 + 256 * b] for b in range(2)]
        actT = [cb[:, 256 * b:256 * (b + 1)].rearrange("p (j n) -> p j n", j=2) for b in range(2)]
        res = [cb[:, 512 + 512 * b:1024 + 512 * b] for b in range(2)]

        eps = stat[:, 60:61]
        zones = [[vb, 512, 2048], [hb, 3072, 4032]]

        def table(*shape):
            n = int(np.prod(shape))
            z = next(z for z in zones if z[1] + n <= z[2])
            z[1] += n
            a = z[0][:, z[1] - n:z[1]]
            if len(shape) == 2:
                a = a.rearrange("p (a b) -> p a b", a=shape[0])
            if len(shape) == 3:
                a = a.rearrange("p (a b c) -> p a b c", a=shape[0], b=shape[1])
            return a

        GE = NE // 4
        logits_zone = hb[:, 3072:3072 + NT * 36].rearrange("p (i n) -> p i n", i=NT)
        zones[1][1] += NT * 36
        R = {name: table(*shape) for name, shape in {
            "gmax": (NT, 1), "dg": (NT, 4), "cand": (NT, 4), "cmin": (NT, 1), "ohg": (NT, 4), "ex4": (NT, 4),
            "gsum": (NT, 1), "gp": (NT, 1), "sel": (NT, 4, GE), "esel": (NT, GE), "m1": (NT, 1), "cand8": (NT, GE),
            "min8": (NT, 1), "oh1": (NT, GE), "e2": (NT, GE), "m2": (NT, 1), "oh2": (NT, GE), "dm": (NT, 1),
            "ex": (NT, 1), "den": (NT, 1), "M1": (NT, 4, GE), "M2": (NT, 4, GE), "oh": (NT, NE), "pos": (NT, NE),
            "row": (NT, NE), "pick": (NT, NE), "cnt": (NE,), "ov": (NE,), "incl": (NE,), "base": (NE,),
            "e64": (NE,), "rowf": (2, NT), "le": (NOV, NE), "eid": (NOV,)}.items()}
        oh = R["oh"]

        def c_(name):
            return prm[:, PRM.index(name)]

        x_in = [sem(f"x_in{i}") for i in range(NT)]
        params_in, consts_in, b_in = sem("params_in"), sem("consts_in"), sem("b_in")
        win_in = [sem(f"win_in{s}") for s in range(2)]
        wb_in = [sem(f"wb_in{s}") for s in range(2)]
        glu_in, router_in = sem("glu_in"), sem("router_in")
        x_again = sem("x_again")
        xc_stored, u8_in, y_stored, yT_in, ker_in = (sem(n) for n in ("xc_stored", "u8_in", "y_stored", "yT_in", "ker_in"))
        bank_full = [sem(f"bank_full{b}") for b in range(8)]
        bank_out = [sem(f"bank_out{b}") for b in range(8)]
        ident_ready, sgw_masked, ldt_spread, consts_made = (sem(n) for n in ("ident_ready", "sgw_masked", "ldt_spread", "consts_made"))
        gp_step, dve_step, act_step = sem("gp_step"), sem("dve_step"), sem("act_step")
        ssq_ready, std_ready, xn_ready = sem("ssq_ready"), sem("std_ready"), sem("xn_ready")
        dt_ready, angle_ready, act_prm = sem("dt_ready"), sem("angle_ready"), sem("act_prm")
        bbar_ready, cp_ready, btpre_ready = sem("bbar_ready"), sem("cp_ready"), sem("btpre_ready")
        var_ready, vstd_ready, vn_ready = sem("var_ready"), sem("vstd_ready"), sem("vn_ready")
        toep_zero, diff_ready, st_ready, tables_ready = sem("toep_zero"), sem("diff_ready"), sem("st_ready"), sem("tables_ready")
        ych_ready, yg_ready, glsig_ready, yc_ready = sem("ych_ready"), sem("yg_ready"), sem("glsig_ready"), sem("yc_ready")
        merge_mul, merge_done, masks_ready = sem("merge_mul"), sem("merge_done"), sem("masks_ready")
        ssq2_ready, std2_ready, h2_ready = sem("ssq2_ready"), sem("std2_ready"), sem("h2_ready")
        h2_stored = [sem(f"h2_stored{i}") for i in range(2)]
        onehot_ready, exp_in, exp_out, exp2_in, exp2_out = (sem(n) for n in ("onehot_ready", "exp_in", "exp_out", "exp2_in", "exp2_out"))
        tok_zero, rows_ready, tok_scattered, tok_in = sem("tok_zero"), sem("rows_ready"), sem("tok_scattered"), sem("tok_in")
        out_stored, gfin_in, sums_ready, ssq3_ready, std3_ready, outrow_ready = (
            sem(n) for n in ("out_stored", "gfin_in", "sums_ready", "ssq3_ready", "std3_ready", "outrow_ready"))
        over_zero = sem("over_zero")
        fin_step, pe_passed, gp_passed = sem("fin_step"), sem("pe_passed"), sem("gp_passed")
        picked = [sem(f"picked{i}") for i in range(2)]
        idx_ready, ov_ready, idx_copied, ov_idx_copied = (sem(n) for n in ("idx_ready", "ov_ready", "idx_copied", "ov_idx_copied"))
        KINDS = ("gate", "up", "down")

        def per_side(name):
            return [sem(f"{name}{b}") for b in range(2)]

        ew_in = [{k: sem(f"{k}_weights_in{b}") for k in KINDS} for b in range(2)]
        done = [{k: sem(f"{k}_done{b}") for k in KINDS} for b in range(2)]
        xg_in, xt_full, xgT_ready, silu_ready = per_side("xg_in"), per_side("xt_full"), per_side("xgT_ready"), per_side("silu_ready")
        act_ready, at_full, actT_ready = per_side("act_ready"), per_side("at_full"), per_side("actT_ready")
        res_ready, res_stored = per_side("res_ready"), per_side("res_stored")
        ov_w, ov_done = sem("ov_weights_in"), {k: sem(f"ov_{k}_done") for k in KINDS}
        (ov_xg_in, ov_xt_full, ov_xgT_ready, ov_silu_ready, ov_act_ready, ov_at_full, ov_actT_ready, ov_res_ready,
         ov_res_stored) = (sem("ov_" + n) for n in ("xg_in", "xt_full", "xgT_ready", "silu_ready", "act_ready",
                                                    "at_full", "actT_ready", "res_ready", "res_stored"))

        def full(eng, name):
            b, n = place[name]
            eng.wait_ge(bank_full[b], n)
            return ps[:, b]

        def taken(eng, name):
            b, n = place[name]
            eng.wait_ge(bank_out[b], n)

        def out_of(name):
            return bank_out[place[name][0]]

        block = ctx.enter_context(nc.Block())


        EW = ({"gate": 2, "up": 3, "down": 4}, {"gate": 5, "up": 0, "down": 1})
        TURNS = NE // 2
        w_src = {"gate": exp_w_gate[0].rearrange("e (p k) n -> e p (k n)", p=P),
                 "up": exp_w_up[0].rearrange("e (p k) n -> e p (k n)", p=P),
                 "down": exp_w_down[0].rearrange("e (k p) n -> e p k n", p=P)}
        B_XT, B_AT, B_GATE, B_UP, B_RES = 0, 1, (2, 3), (4, 5), (6, 7)
        xt_bank = ps[:, B_XT].rearrange("p (k t) -> p k t", k=KD)
        at_bank = ps[:, B_AT, 0:256].rearrange("p (j n) -> p j n", j=2)
        HALF = F // 2

        def weights(eng, b, kind, e, signal):
            src = w_src[kind][e] if isinstance(e, int) else w_src[kind][bass.ds(e, 1)]
            dst = ring[:, EW[b][kind]]
            if kind == "down":
                dst = slot_h[EW[b][kind]]
                if not isinstance(e, int):
                    src = src.rearrange("e p k n -> p (e k) n")
            elif not isinstance(e, int):
                src = src.rearrange("e p n -> (e p) n")
            eng.dma_start(dst, src).then_inc(signal, 16)

        def turn_x(pe, b):
            pe.sem_inc(pe_passed, 1)
            v = xg[b].rearrange("t (p k) -> t k p", k=KD)
            for k in range(KD):
                t = nc.tensor.transpose(xt_bank[:, k], v[:, k], ident[0:CAP, 0:CAP])
            return t

        def hidden(b, kind, bank):
            w = slot_k[EW[b][kind]]
            for k in range(KD):
                for h in range(2):
                    t = nc.tensor.matmul(ps[CAP * h:CAP * (h + 1), bank, 0:HALF], xgT[b][:, k],
                                         w[:, k, HALF * h:HALF * (h + 1)], start=k == 0, stop=k == KD - 1)
            return t

        def turn_act(b):
            for j in range(2):
                t = nc.tensor.transpose(at_bank[:, j], act_[b][:, P * j:P * (j + 1)], ident[:])
            return t

        def down(b, bank):
            w = slot_h[EW[b]["down"]]
            for n, (h, j) in enumerate((h, j) for h in range(2) for j in range(2)):
                for c in range(2):
                    t = nc.tensor.matmul(ps[CAP * c:CAP * (c + 1), bank], actT[b][:, j, CAP * h:CAP * (h + 1)],
                                         w[:, 2 * h + j, W * c:W * (c + 1)], start=n == 0, stop=n == 3)
            return t

        def gain(b):
            return nc.vector.tensor_tensor(xgT[b], xt_bank, cols[:, GFX:GFX + KD].unsqueeze(2).to_broadcast((P, KD, CAP)), ALU.mult)

        def store_rows(eng, b, block, signal):
            for c in range(2):
                eng.dma_start(res_d[bass.ds(block * CAP, CAP), W * c:W * (c + 1)],
                              res[b][CAP * c:CAP * (c + 1)]).then_inc(signal, 16)

        def n_over(eng):
            eng.wait_ge(ov_ready, 1)
            return eng.value_load(ovi[0:1, 15:16], min_val=0, max_val=NOV)

        def each_over(eng, body):
            n = n_over(eng)
            with eng.If(n > 0):
                body(0, True)
            with eng.Fori(1, NOV) as o_:
                with eng.If(n > o_):
                    body(o_, False)
            return n

        def experts_sync(sp):
            sp.wait_ge(yc_ready, MW)
            for kind in KINDS:
                weights(sp, 0, kind, 0, ew_in[0][kind])
            full(sp, ("br", 5, MW - 1))
            weights(sp, 1, "gate", 1, ew_in[1]["gate"])
            full(sp, ("o", NT - 1, 1))
            for kind in ("up", "down"):
                weights(sp, 1, kind, 1, ew_in[1][kind])
            for s in range(2):
                sp.wait_ge(h2_stored[s], 16 * 2)
            full(sp, ("rt", NT - 1, 1))
            sp.dma_start(hb[:, 0:D], norm_final_g.rearrange("(a d) -> a d", a=1).to_broadcast((P, D))).then_inc(gfin_in, 16)
            with sp.Fori(1, TURNS) as i:
                for b in range(2):
                    for kind in KINDS:
                        sp.wait_ge(done[b][kind], i)
                        weights(sp, b, kind, i * 2 + b, ew_in[b][kind])
            for kind in KINDS:
                sp.wait_ge(done[0][kind], TURNS)

            def over(o_, first):
                e = sp.value_load(ovi[0:1, bass.ds(o_, 1)] if not first else ovi[0:1, 0:1], min_val=0, max_val=NE - 1)
                for kind in KINDS:
                    if not first:
                        sp.wait_ge(ov_done[kind], o_)
                    weights(sp, 0, kind, e, ov_w)

            each_over(sp, over)
            for i in range(NT):
                sp.wait_ge(outrow_ready, i + 1)
                sp.dma_start(out[0, i * P:(i + 1) * P, :], x3[:, i]).then_inc(out_stored, 16)
            sp.wait_ge(out_stored, 16 * NT)

        def experts_tensor(pe):
            for b in range(8):
                pe.wait_ge(bank_out[b], max(n for bank, n in place.values() if bank == b))
            pe.wait_ge(xg_in[0], 16)
            turn_x(pe, 0).then_inc(xt_full[0], 1)

            def turn(i, first):
                for b in range(2):
                    for kind, bank in (("gate", B_GATE[b]), ("up", B_UP[b])):
                        pe.wait_ge(ew_in[b][kind], i * 16 + 16)
                        if kind == "gate":
                            pe.wait_ge(xgT_ready[b], i + 1)
                            if not first:
                                pe.wait_ge(act_ready[b], i)
                        hidden(b, kind, bank).then_inc(done[b][kind], 1)
                    pe.wait_ge(xg_in[1 - b], i * 16 + 16 + 16 * b)
                    turn_x(pe, 1 - b).then_inc(xt_full[1 - b], 1)
                    pe.wait_ge(act_ready[b], i + 1)
                    turn_act(b).then_inc(at_full[b], 1)
                    pe.wait_ge(actT_ready[b], i + 1)
                    pe.wait_ge(ew_in[b]["down"], i * 16 + 16)
                    if not first:
                        pe.wait_ge(res_ready[b], i)
                    down(b, B_RES[b]).then_inc(done[b]["down"], 1)

            turn(0, True)
            with pe.Fori(1, TURNS) as i:
                turn(i, False)

            def over(o_, first):
                pe.wait_ge(ov_xg_in, o_ * 16 + 16)
                if first:
                    pe.wait_ge(xgT_ready[0], TURNS + 1)
                turn_x(pe, 0).then_inc(ov_xt_full, 1)
                pe.wait_ge(ov_w, o_ * 48 + 48)
                pe.wait_ge(ov_xgT_ready, o_ + 1)
                if first:
                    pe.wait_ge(res_ready[0], TURNS)
                hidden(0, "gate", B_GATE[0]).then_inc(ov_done["gate"], 1)
                hidden(0, "up", B_UP[0]).then_inc(ov_done["up"], 1)
                pe.wait_ge(ov_act_ready, o_ + 1)
                turn_act(0).then_inc(ov_at_full, 1)
                pe.wait_ge(ov_actT_ready, o_ + 1)
                if not first:
                    pe.wait_ge(ov_res_ready, o_)
                down(0, B_RES[0]).then_inc(ov_done["down"], 1)

            each_over(pe, over)

        def experts_vector(v):
            v.wait_ge(xt_full[0], 1)
            gain(0).then_inc(xgT_ready[0], 1)

            def turn(i, first):
                for b in range(2):
                    v.wait_ge(silu_ready[b], i + 1)
                    v.wait_ge(done[b]["up"], i + 1)
                    if not first:
                        v.wait_ge(at_full[b], i)
                    nc.vector.tensor_tensor(act_[b], silu[b], ps[:, B_UP[b], 0:HALF], ALU.mult).then_inc(act_ready[b], 1)
                    v.wait_ge(xt_full[1 - b], i + 1 + b)
                    if b == 1 or not first:
                        v.wait_ge(done[1 - b]["up"], i + b)
                    gain(1 - b).then_inc(xgT_ready[1 - b], 1)
                    v.wait_ge(at_full[b], i + 1)
                    if not first:
                        v.wait_ge(done[b]["down"], i)
                    nc.vector.tensor_copy(actT[b], at_bank).then_inc(actT_ready[b], 1)

            turn(0, True)
            with v.Fori(1, TURNS) as i:
                turn(i, False)

            def over(o_, first):
                v.wait_ge(ov_xt_full, o_ + 1)
                if first:
                    v.wait_ge(done[0]["up"], TURNS)
                gain(0).then_inc(ov_xgT_ready, 1)
                v.wait_ge(ov_silu_ready, o_ + 1)
                v.wait_ge(ov_done["up"], o_ + 1)
                nc.vector.tensor_tensor(act_[0], silu[0], ps[:, B_UP[0], 0:HALF], ALU.mult).then_inc(ov_act_ready, 1)
                v.wait_ge(ov_at_full, o_ + 1)
                if first:
                    v.wait_ge(done[0]["down"], TURNS)
                nc.vector.tensor_copy(actT[0], at_bank).then_inc(ov_actT_ready, 1)

            each_over(v, over)
            v.wait_ge(gfin_in, 16)
            for i in range(NT):
                rows = [mb[:, 2048 * (i % 2) + 1024 * c:2048 * (i % 2) + 1024 * (c + 1)] for c in range(2)]
                v.wait_ge(picked[i % 2], 32 * (i // 2 + 1))
                for c in range(2):
                    s = nc.vector.scalar_tensor_tensor(x3[:, i], rows[c], wts[:, NT * c + i:NT * c + i + 1], x3[:, i],
                                                       ALU.mult, ALU.add)
                    s.then_inc(sums_ready, 1)
                    v.wait_ge(sums_ready, 2 * i + c + 1)
                v.wait_ge(std3_ready, i + 1)
                nc.vector.reciprocal(stat[:, 24 + i:25 + i], stat[:, 20 + i:21 + i]).then_inc(fin_step, 1)
                v.wait_ge(fin_step, i + 1)
                nc.vector.scalar_tensor_tensor(x3[:, i], x3[:, i], stat[:, 24 + i:25 + i], hb[:, 0:D],
                                               ALU.mult, ALU.mult).then_inc(outrow_ready, 1)

        def experts_scalar(act):
            def results(b, block, full_sem, full_n, ready, ready_n, stored, stored_n):
                act.wait_ge(full_sem, full_n)
                if stored_n is not None:
                    act.wait_ge(stored, stored_n)
                nc.scalar.copy(res[b], ps[:, B_RES[b]]).then_inc(ready, 1)
                act.wait_ge(ready, ready_n)
                store_rows(act, b, block, stored)

            def turn(i, first):
                for b in range(2):
                    act.wait_ge(done[b]["gate"], i + 1)
                    if not first:
                        act.wait_ge(act_ready[b], i)
                    nc.scalar.activation(silu[b], ps[:, B_GATE[b], 0:HALF], ACT.Silu).then_inc(silu_ready[b], 1)
                    results(b, i * 2 + b, done[b]["down"], i + 1, res_ready[b], i + 1, res_stored[b], None if first else i * 32)

            turn(0, True)
            with act.Fori(1, TURNS) as i:
                turn(i, False)

            def over(o_, first):
                act.wait_ge(ov_done["gate"], o_ + 1)
                if first:
                    act.wait_ge(act_ready[0], TURNS)
                else:
                    act.wait_ge(ov_act_ready, o_)
                nc.scalar.activation(silu[0], ps[:, B_GATE[0], 0:HALF], ACT.Silu).then_inc(ov_silu_ready, 1)
                if first:
                    act.wait_ge(res_stored[0], TURNS * 32)
                results(0, o_ + NE, ov_done["down"], o_ + 1, ov_res_ready, o_ + 1, ov_res_stored, None if first else o_ * 32)

            each_over(act, over)
            for i in range(NT):
                act.wait_ge(sums_ready, 2 * i + 2)
                nc.scalar.activation(ring[:, 0, 0:D], x3[:, i], ACT.Square, accum_out=stat[:, 16 + i:17 + i]).then_inc(ssq3_ready, 1)
                act.wait_ge(ssq3_ready, i + 1)
                nc.scalar.activation(stat[:, 20 + i:21 + i], stat[:, 16 + i:17 + i], ACT.Sqrt, scale=1.0 / D,
                                     bias=eps).then_inc(std3_ready, 1)

        def gather_rows(dst, table_, idx, signal):
            nc.gpsimd.indirect_dma_start(dst, None, table_, bass.IndirectOffsetOnAxis(ap=idx, axis=0)).then_inc(signal, 16)

        def experts_gpsimd(gp):
            gp.wait_ge(idx_ready, 1)
            for s in range(2):
                gp.wait_ge(h2_stored[s], 16 * 2)

            def fetch(e, b, count, signal, copied, side):
                src = idx_u[:, e:e + 1] if isinstance(e, int) else idx_u[:, bass.ds(e, 1)]
                nc.gpsimd.tensor_copy(idx_now[:, side:side + 1], src).then_inc(copied, 1)
                gp.wait_ge(copied, count)
                gp.sem_inc(gp_passed, 1)
                gather_rows(xg[b], h2_d, idx_now[:, side:side + 1], signal)

            for b in range(2):
                fetch(b, b, b + 1, xg_in[b], idx_copied, b)
            with gp.Fori(1, TURNS) as i:
                for b in range(2):
                    gp.wait_ge(xt_full[b], i)
                    fetch(i * 2 + b, b, i * 2 + b + 1, xg_in[b], idx_copied, b)
            gp.wait_ge(xt_full[0], TURNS)
            fetch(NE, 0, NE + 1, xg_in[0], idx_copied, 0)
            gp.wait_ge(xt_full[0], TURNS + 1)

            def over(o_, first):
                if not first:
                    gp.wait_ge(ov_xt_full, o_)
                fetch(o_ + NE, 0, o_ + 1, ov_xg_in, ov_idx_copied, 2)

            n = each_over(gp, over)
            for b in range(2):
                gp.wait_ge(res_stored[b], TURNS * 32)
            with gp.If(n > 0):
                gp.wait_ge(ov_res_stored, n * 32)
                gp.sem_inc(gp_passed, 1)
            for i in range(NT):
                if i >= 2:
                    gp.wait_ge(sums_ready, 2 * (i - 2) + 2)
                for c in range(2):
                    gather_rows(mb[:, 2048 * (i % 2) + 1024 * c:2048 * (i % 2) + 1024 * (c + 1)], res_d,
                                row_u[:, NT * c + i:NT * c + i + 1], picked[i % 2])

        @block.sync
        def _(sp):
            for i, a in enumerate((ssm_a_re, ssm_a_im)):
                sp.dma_start(par_nat[:, i].rearrange("q (two p) -> q two p", two=2),
                             a[0].rearrange("(two q) p -> q two p", two=2)).then_inc(params_in, 16)
            sp.dma_start(ldt_nat, ssm_log_dt[0].rearrange("(two q) -> q two", two=2)).then_inc(params_in, 16)
            for r, c in enumerate((ssm_c_re, ssm_c_im)):
                for t in range(2):
                    sp.dma_start(c_nat[r][:, t].rearrange("p (two s) -> p two s", two=2),
                                 c[0].rearrange("(two t q) c s -> t (q c) two s", two=2, t=2)[t]).then_inc(params_in, 16)
            sp.dma_start(sgw_nat, sgu_w[0].rearrange("h t s -> t h s")).then_inc(params_in, 16)
            for i in range(NT):
                sp.dma_start(x3[:, i], x[0, i * P:(i + 1) * P, :]).then_inc(x_in[i], 16)

            def load_win(n, last=None):
                if last:
                    full(sp, last)
                src = (w_in[0][:, WIN_COLS[n]:WIN_COLS[n] + W] if n < 10 else w_out[0][:, (n - 10) * W:(n - 9) * W])
                sp.dma_start(slot_k[n % 2], src.rearrange("(k p) n -> p k n", p=P)).then_inc(win_in[n % 2], 16)

            def load_wb(n, last):
                half, k = GATE_STEPS[n]
                full(sp, last)
                sp.dma_start(wb_slot[n % 2], w_branch[0, k][:, half * W:(half + 1) * W].rearrange(
                    "(k p) n -> p k n", p=P)).then_inc(wb_in[n % 2], 16)

            sp.dma_start(cols[:, GMX:GMX + KD], norm_mix_g[0].rearrange("(k p) -> p k", p=P)).then_inc(b_in, 16)
            for r, b in enumerate((ssm_b_re, ssm_b_im)):
                for two in range(2):
                    sp.dma_start(b_raw[r][two * S:(two + 1) * S],
                                 b[0, two * Q:(two + 1) * Q].rearrange("q s c -> s q c")).then_inc(b_in, 16)
            load_win(0)
            load_win(1)
            sp.dma_start(cols[:, BG:BG + 24], b_gate[0].rearrange("(k p) -> p k", p=P)).then_inc(consts_in, 16)
            for at, v, k in ((GB, glu_b, 4), (PSC, pool_scale, 4), (DSK, ssm_d, 4), (GFF, norm_ffn_g, KD)):
                sp.dma_start(cols[:, at:at + k], v[0].rearrange("(k p) -> p k", p=P)).then_inc(consts_in, 16)
            sp.dma_start(cols[:, GFX:GFX + KD], norm_ffn_g[0].rearrange("(p k) -> p k", p=P)).then_inc(consts_in, 16)
            sp.dma_start(poolw[:], pool_w[0].rearrange("g c d -> c g d")).then_inc(consts_in, 16)
            sp.dma_start(bs_row[:], sgu_b[0:1]).then_inc(consts_in, 16)
            sp.dma_start(rbias[:, 0:4], router_group_b[0:1]).then_inc(consts_in, 16)
            sp.dma_start(rbias[:, 4:36], router_expert_b[0:1]).then_inc(consts_in, 16)
            sp.dma_start(lng[:], sgu_ln_g[0:1].to_broadcast((P, W))).then_inc(consts_in, 16)
            sp.dma_start(lnb[:], sgu_ln_b[0:1].to_broadcast((P, W))).then_inc(consts_in, 16)

            taken(sp, ("c", MW - 1))
            sp.dma_start(xc_d.rearrange("(m p) t -> p m t", p=P), C).then_inc(xc_stored, 16)
            load_win(2, ("c", MW - 1))
            sp.wait_ge(xc_stored, 16)
            for j in range(J):
                sp.dma_start(u8v[CH * j:CH * (j + 1)],
                             xc_d.rearrange("(g c) (j n) -> j c g n", c=CH, j=J)[j]).then_inc(u8_in, 16)
            load_win(3, ("v", NT - 1))
            taken(sp, ("k", 7))
            sp.wait_ge(toep_zero, 1)
            over_rows = res_d[NE * CAP:, :].rearrange("(p h r) d -> h p (r d)", h=2, r=4)
            for h in range(2):
                sp.dma_start(over_rows[h], xb[0:NOV * CAP // 8, :]).then_inc(over_zero, 16)
            sp.wait_ge(over_zero, 32)
            for i in range(J):
                sp.dma_start(toep[CH * i:CH * (i + 1), :, CH * i:P], ker[:, :, 0:P - CH * i]).then_inc(ker_in, 16)
            sp.wait_ge(ker_in, 16 * J)
            sp.dma_start(gluw, glu_w[0].rearrange("(k p) n -> p k n", p=P)).then_inc(glu_in, 16)
            load_win(4, ("a", MW - 1))
            load_wb(0, ("bu", 1, 1))
            load_wb(1, ("bu", 1, 1))
            load_win(5, ("u", MW - 1))
            full(sp, ("sg", 3))
            sp.dma_start(rw[:, :, 0:4], router_group_w[0].rearrange("(k p) n -> p k n", p=P)).then_inc(router_in, 16)
            sp.dma_start(rw[:, :, 4:36], router_expert_w[0].rearrange("(k p) n -> p k n", p=P)).then_inc(router_in, 16)
            full(sp, ("y", 3))
            sp.dma_start(x3, x[0].rearrange("(i p) d -> p i d", p=P)).then_inc(x_again, 16)
            taken(sp, ("y", 3))
            for j in range(J):
                sp.dma_start(y_d.rearrange("(g c) (j n) -> j c g n", c=CH, j=J)[j],
                             y8v[CH * j:CH * (j + 1)]).then_inc(y_stored, 16)
            sp.wait_ge(y_stored, 16 * J)
            sp.dma_start(yT, y_d.rearrange("(m p) t -> p m t", p=P)).then_inc(yT_in, 16)
            for n in range(2, 6):
                load_win(4 + n, ("gt", n - 2, MW - 1))
                load_wb(n, ("br", n - 2, MW - 1))
            load_win(10, ("gt", 4, MW - 1))
            load_win(11, ("gt", 5, MW - 1))
            experts_sync(sp)

        @block.tensor
        def _(pe):
            def start(name):
                b, n = place[name]
                if n > 1:
                    pe.wait_ge(bank_out[b], n - 1)
                return ps[:, b]

            def end(name, ins):
                ins.then_inc(bank_full[place[name][0]], 1)

            def turn(name, ins_, ready=None):
                bank, at = start(name), 0
                for a in ins_:
                    n, w = a.shape[0], a.shape[1]
                    t = nc.tensor.transpose(bank[0:w, at:at + n], a, ident[0:n, 0:n])
                    at += n
                end(name, t)

            def product(name, pairs, cols_=512):
                bank = start(name)
                for i, (lhs, rhs) in enumerate(pairs):
                    t = nc.tensor.matmul(bank[0:lhs.shape[1], 0:cols_], lhs, rhs, start=i == 0, stop=i == len(pairs) - 1)
                end(name, t)

            pe.wait_ge(ident_ready, 1)
            pe.wait_ge(params_in, 16 * 8)
            pe.wait_ge(ldt_spread, 1)
            turn("par", [par_nat[:, i] for i in range(3)])
            turn("ct", [c_nat[r][:, t] for r in range(2) for t in range(2)])
            pe.wait_ge(sgw_masked, 1)
            turn("wst", [sgw_nat[:, h] for h in range(4)])
            for i in range(NT):
                pe.wait_ge(xn_ready, i + 1)
                for h in range(2):
                    turn(("x", i, h), [x3[:, i, (4 * h + k) * P:(4 * h + k + 1) * P] for k in range(4)])
            taken(pe, ("x", NT - 1, 1))

            def channels(tag, n):
                pe.wait_ge(win_in[n % 2], 16 * (n // 2 + 1))
                for m in range(MW):
                    product((*tag, m), [(slot_k[n % 2][:, k, m * P:(m + 1) * P], hT[:, k]) for k in range(KD)])

            channels(("c",), 0)
            pe.wait_ge(win_in[1], 16)
            for i in range(NT):
                product(("v", i), [(hT[:, k, i * P:(i + 1) * P], slot_k[1][:, k]) for k in range(KD)])
            pe.wait_ge(btpre_ready, 1)
            for r in range(2):
                for i in range(4):
                    turn(("bt", r, i), [bt_pre[r][:, q].rearrange("p j c -> p (j c)") for q in range(4 * i, 4 * i + 4)])
            pe.wait_ge(cp_ready, 1)
            for i in range(8):
                bank = start(("k", i))
                for g in range(4 * i, 4 * i + 4):
                    rows, q = slice(S * (g // Q), S * (g // Q + 1)), g % Q
                    o_ = bank[0:CH, P * (g % 4):P * (g % 4 + 1)]
                    nc.tensor.matmul(o_, b_bar[0][rows, q], cp_re[rows, q, 0:J].rearrange("p j c -> p (j c)"), start=True, stop=False)
                    t = nc.tensor.matmul(o_, b_bar[1][rows, q], cp_im[rows, q, 0:J].rearrange("p j c -> p (j c)"), start=False, stop=True)
                end(("k", i), t)
            channels(("a",), 2)
            pe.wait_ge(u8_in, 16 * J)
            taken(pe, ("bt", 1, 3))
            for h in range(2):
                for r in range(2):
                    bank = start(("bu", h, r))
                    for q in range(8 * h, 8 * h + 8):
                        for two in range(2):
                            t = nc.tensor.matmul(bank[S * two:S * (two + 1), NC * (q % 8):NC * (q % 8 + 1)],
                                                 btT[r][:, q, S * two:S * (two + 1)], u8v[:, two * Q + q], start=True, stop=True)
                    end(("bu", h, r), t)
            channels(("u",), 3)
            pe.wait_ge(consts_in, 16 * 12)
            for m in range(MW):
                pe.wait_ge(diff_ready, m + 1)
                product(("py", m), [(poolw[:, m], A[:, m])])
            pe.wait_ge(vn_ready, NT)
            pe.wait_ge(consts_made, 1)
            for h in range(4):
                bank = start(("sg", h))
                for n in range(NT):
                    nc.tensor.matmul(bank[:, n * P:(n + 1) * P], ones_row[:], bs_row[0:1, h], start=True, stop=False)
                    t = nc.tensor.matmul(bank[:, n * P:(n + 1) * P], V[:, n, h * P:(h + 1) * P], wst[:, h], start=False, stop=True)
                end(("sg", h), t)
            pe.wait_ge(ker_in, 16 * J)
            pe.wait_ge(st_ready, 1)
            for i in range(4):
                bank = start(("y", i))
                for g in range(8 * i, 8 * i + 8):
                    rows, q = slice(S * (g // Q), S * (g // Q + 1)), g % Q
                    o_ = bank[:, NC * (g % 8):NC * (g % 8 + 1)]
                    nc.tensor.matmul(o_, toep[:, g], u8v[:, g], start=True, stop=False)
                    nc.tensor.matmul(o_, cp_re[rows, q, 1:J + 1].rearrange("p j c -> p (j c)"), st_re[rows, q], start=False, stop=False)
                    t = nc.tensor.matmul(o_, cp_im[rows, q, 1:J + 1].rearrange("p j c -> p (j c)"), st_im[rows, q], start=False, stop=True)
                end(("y", i), t)
            for n, (half, k_) in enumerate(GATE_STEPS):
                pe.wait_ge(win_in[n % 2], 16 * ((4 + n) // 2 + 1))
                pe.wait_ge(wb_in[n % 2], 16 * (n // 2 + 1))
                if n == 0:
                    taken(pe, ("py", MW - 1))
                elif n == 1:
                    taken(pe, ("sg", 3))
                elif n == 2:
                    pe.wait_ge(yc_ready, MW)
                Y = (A, U, C)[k_]
                for m in range(MW):
                    ms = slice(m * P, (m + 1) * P)
                    product(("gt", n, m), [(slot_k[n % 2][:, k, ms], hT[:, k]) for k in range(KD)])
                    product(("br", n, m), [(wb_slot[n % 2][:, k, ms], Y[:, k]) for k in range(MW)])
                if n == 1:
                    pe.wait_ge(glu_in, 16)
                    pe.wait_ge(yg_ready, MW)
                    for m in range(MW):
                        product(("gl", m), [(gluw[:, k, m * P:(m + 1) * P], C[:, k]) for k in range(MW)])
            taken(pe, ("br", 5, MW - 1))
            for s in range(2):
                pe.wait_ge(win_in[s], 16 * 6)

            def route(i):
                pe.wait_ge(h2_ready, i + 1)
                for h in range(2):
                    turn(("rt", i, h), [h2n[i % 2][:, (4 * h + k) * P:(4 * h + k + 1) * P] for k in range(4)])
                taken(pe, ("rt", i, 1))
                product(("lg", i), [(h2T[:, k], rw[:, k]) for k in range(KD)] + [(ones_row[:], rbias[:])], 36)

            pe.wait_ge(router_in, 32)
            for i in range(NT):
                for h in range(2):
                    product(("o", i, h), [(M[:, k, i * P:(i + 1) * P], slot_k[h][:, k]) for k in range(KD)])
                if i >= 1:
                    route(i - 1)
            route(NT - 1)
            pe.wait_ge(onehot_ready, 1)
            pe.wait_ge(masks_ready, 1)
            bank = start("pos")
            tri, ones = lng[:, 0:P], lnb[:, 0:P]
            for i in range(NT):
                for i2 in range(i + 1):
                    nc.tensor.matmul(bank[:, NE * i:NE * (i + 1)], tri if i2 == i else ones, oh[:, i2], start=i2 == 0, stop=i2 == i)
            for i in range(NT):
                t = nc.tensor.matmul(bank[:, NE * NT:NE * (NT + 1)], ones, oh[:, i], start=i == 0, stop=i == NT - 1)
            end("pos", t)
            pe.wait_ge(tok_in, 16)
            turn("tok", [tok_rows])
            experts_tensor(pe)

        @block.scalar
        def _(act):
            step = Steps(act, act_step)

            def copy_out(name, dst, rows=P, cols_=512):
                nc.scalar.copy(dst, full(act, name)[0:rows, 0:cols_]).then_inc(out_of(name), 1)

            copy_out("par", prm[:, 0:3].rearrange("p n q -> p (n q)"), cols_=48)
            copy_out("ct", ub[:, 1024:1536])
            taken(act, "par")
            nc.scalar.activation(c_("dt"), c_("ldt"), ACT.Exp).then_inc(dt_ready, 1)
            for i in range(NT):
                act.wait_ge(x_in[i], 16)
                nc.scalar.activation(mb[:, 1024 * i:1024 * (i + 1)], x3[:, i], ACT.Square,
                                     accum_out=stat[:, i:i + 1]).then_inc(ssq_ready, 1)
            act.wait_ge(ssq_ready, NT)
            act.wait_ge(consts_made, 1)
            nc.scalar.activation(stat[:, 4:8], stat[:, 0:4], ACT.Sqrt, scale=1.0 / D, bias=eps).then_inc(std_ready, 1)
            act.wait_ge(angle_ready, 1)
            nc.scalar.activation(c_("e1"), c_("r"), ACT.Exp).then_inc(act_prm, 1)
            nc.scalar.activation(c_("rho"), c_("r"), ACT.Exp, scale=float(J)).then_inc(act_prm, 1)
            nc.scalar.activation(c_("tanh"), c_("r"), ACT.Tanh, scale=0.5).then_inc(act_prm, 1)
            nc.scalar.activation(c_("s"), c_("nhalf"), ACT.Sin).then_inc(act_prm, 1)
            nc.scalar.activation(c_("c"), c_("ab"), ACT.Sin).then_inc(act_prm, 1)
            copy_out("wst", wst[:].rearrange("p h t -> p (h t)"))
            for m in range(MW):
                name = ("c", m)
                nc.scalar.copy(C[:, m].rearrange("p (j c) -> p c j", j=J),
                               full(act, name).rearrange("p (c j) -> p c j", j=J)).then_inc(out_of(name), 1)
            for i in range(NT):
                name = ("v", i)
                nc.scalar.activation(V[:, i], full(act, name), ACT.Gelu_apprx_tanh).then_inc(out_of(name), 1)
            act.wait_ge(var_ready, 1)
            nc.scalar.activation(stat[:, 40:44], stat[:, 32:36], ACT.Sqrt, bias=eps).then_inc(vstd_ready, 1)
            for r in range(2):
                for i in range(4):
                    copy_out(("bt", r, i), btT[r][:, 4 * i:4 * i + 4].rearrange("p q n -> p (q n)"))
            for i in range(8):
                copy_out(("k", i), ker[:, 4 * i:4 * i + 4].rearrange("p g n -> p (g n)"), rows=CH)
            for m in range(MW):
                copy_out(("a", m), A[:, m])
            for m in range(MW):
                name = ("u", m)
                nc.scalar.activation(U[:, m], full(act, name), ACT.Gelu_apprx_tanh).then_inc(out_of(name), 1)
            act.wait_ge(consts_in, 16 * 12)
            for m in range(MW):
                name = ("py", m)
                nc.scalar.activation(A[:, m], full(act, name), ACT.Copy, scale=cols[:, PSC + m:PSC + m + 1]).then_inc(out_of(name), 1)
            act.wait_ge(st_ready, 1)
            for i in range(4):
                copy_out(("y", i), y8v[:, 8 * i:8 * i + 8].rearrange("p g c -> p (g c)"))
            for n, (half, k_) in enumerate(GATE_STEPS):
                for m in range(MW):
                    i = n * MW + m
                    col = BG + k_ * KD + half * MW + m
                    if i >= 2:
                        act.wait_ge(merge_done, i - 1)
                    name = ("gt", n, m)
                    bank = full(act, name)
                    nc.scalar.activation(sig[i % 2], bank, ACT.Sigmoid, bias=cols[:, col:col + 1]).then_inc(out_of(name), 1)
                if n == 0:
                    for m in range(MW):
                        act.wait_ge(ych_ready, m + 1)
                        nc.scalar.activation(C[:, m].rearrange("p (c j) -> p c j", j=J),
                                             yT[:, m].rearrange("p (j c) -> p c j", j=J), ACT.Gelu_apprx_tanh).then_inc(yg_ready, 1)
                if n == 1:
                    for m in range(MW):
                        name = ("gl", m)
                        bank = full(act, name)
                        if m == 0:
                            act.wait_ge(yg_ready, MW)
                        nc.scalar.activation(yT[:, m], bank, ACT.Sigmoid, bias=cols[:, GB + m:GB + m + 1]).then_inc(out_of(name), 1)
            for i in range(NT):
                taken(act, ("o", i, 1))
                nc.scalar.activation(cb[:, 0:1024], x3[:, i], ACT.Square, accum_out=stat[:, 8 + i:9 + i]).then_inc(ssq2_ready, 1)
                act.wait_ge(ssq2_ready, i + 1)
                nc.scalar.activation(stat[:, 12 + i:13 + i], stat[:, 8 + i:9 + i], ACT.Sqrt, scale=1.0 / D,
                                     bias=eps).then_inc(std2_ready, 1)
            act.wait_ge(exp_in, 1)
            nc.scalar.activation(R["ex4"], R["dg"], ACT.Exp).then_inc(exp_out, 1)
            act.wait_ge(exp2_in, 1)
            nc.scalar.activation(R["ex"], R["dm"], ACT.Exp).then_inc(exp2_out, 1)
            experts_scalar(act)

        @block.vector
        def _(v):
            vv = nc.vector
            step = Steps(v, dve_step)
            then, mark = step.then, step.mark

            def mul(o_, a, b):
                return vv.tensor_tensor(o_, a, b, ALU.mult)

            def add(o_, a, b):
                return vv.tensor_tensor(o_, a, b, ALU.add)

            def sub(o_, a, b):
                return vv.tensor_tensor(o_, a, b, ALU.subtract)

            def axpy(o_, a, k, b, op=ALU.add):
                return vv.scalar_tensor_tensor(o_, a, k, b, ALU.mult, op)

            def cmul(o_re, o_im, a, b, t, conj=False, neg_im=False):
                mark(mul(t, a[1], b[1]))
                then(mul(o_re, a[0], b[0]))
                then((add if conj else sub)(o_re, o_re, t))
                mark(mul(t, a[0], b[1]))
                then(mul(o_im, a[1], b[0]))
                if neg_im:
                    then(axpy(o_im, o_im, -1.0, t, ALU.subtract))
                else:
                    then((sub if conj else add)(o_im, o_im, t))

            C1 = 6.28125
            C2 = 0.0019350051879882812
            C3 = 2 * math.pi - C1 - C2
            taken(v, "par")
            v.wait_ge(dt_ready, 1)
            mark(mul(c_("r"), c_("are"), c_("dt")))
            then(mul(c_("th"), c_("aim"), c_("dt")))
            then(vv.tensor_scalar(c_("n"), c_("th"), 1.0 / (2 * math.pi), MAGIC, ALU.mult, ALU.add))
            then(vv.tensor_scalar(c_("n2"), c_("n"), -MAGIC, None, ALU.add))
            then(axpy(c_("t1"), c_("n2"), -C1, c_("th")))
            then(axpy(c_("t2"), c_("n2"), -C2, c_("t1")))
            then(axpy(c_("thr"), c_("n2"), -C3, c_("t2")))
            then(vv.tensor_scalar(c_("nhalf"), c_("thr"), 0.5, None, ALU.mult))
            then(axpy(c_("t3"), c_("nhalf"), -1.0, c_("nhalf"), ALU.max))
            vv.tensor_scalar(c_("ab"), c_("t3"), -1.0, math.pi / 2, ALU.mult, ALU.add).then_inc(angle_ready, 1)
            mark(mul(c_("t1"), c_("are"), c_("are")))
            then(mul(c_("t2"), c_("aim"), c_("aim")))
            then(add(c_("m2"), c_("t1"), c_("t2")))
            then(vv.reciprocal(c_("inv"), c_("m2")))

            v.wait_ge(std_ready, 1)
            then(vv.reciprocal(stat[:, 28:32], stat[:, 4:8]))
            v.wait_ge(b_in, 16 * 5)

            def spread_out(i):
                for h in range(2):
                    name = ("x", i, h)
                    bank = full(v, name).rearrange("p (k t) -> p k t", k=4)
                    vv.tensor_tensor(hT[:, 4 * h:4 * h + 4, i * P:(i + 1) * P], bank,
                                     cols[:, GMX + 4 * h:GMX + 4 * h + 4].unsqueeze(2).to_broadcast((P, 4, P)),
                                     ALU.mult).then_inc(out_of(name), 1)

            for i in range(NT):
                vv.tensor_scalar(x3[:, i], x3[:, i], stat[:, 28 + i:29 + i], None, ALU.mult).then_inc(xn_ready, 1)
                if i >= 1:
                    spread_out(i - 1)
            spread_out(NT - 1)

            v.wait_ge(act_prm, 5)
            mark(vv.tensor_scalar(c_("one_m"), c_("tanh"), -1.0, 1.0, ALU.mult, ALU.add))
            mark(vv.scalar_tensor_tensor(c_("cosm1"), c_("s"), -2.0, c_("s"), ALU.mult, ALU.mult))
            then(vv.scalar_tensor_tensor(c_("sin"), c_("s"), 2.0, c_("c"), ALU.mult, ALU.mult))
            mark(vv.reciprocal(c_("t1"), c_("one_m")))
            then(vv.tensor_scalar(c_("cos"), c_("cosm1"), 1.0, None, ALU.add))
            mark(vv.memset(pw_re[:, 0], 1.0))
            mark(vv.memset(pw_im[:, 0], 0.0))
            mark(mul(pw_re[:, 1], c_("e1"), c_("cos")))
            mark(mul(pw_im[:, 1], c_("e1"), c_("sin")))
            then(vv.scalar_tensor_tensor(c_("em1"), c_("tanh"), 2.0, c_("t1"), ALU.mult, ALU.mult))
            then(mul(c_("t2"), c_("em1"), c_("cos")))
            then(add(c_("nr"), c_("t2"), c_("cosm1")))
            cmul(c_("t1"), c_("t2"), (c_("nr"), pw_im[:, 1]), (c_("are"), c_("aim")), c_("t3"), conj=True)
            mark(mul(c_("wr"), c_("t1"), c_("inv")))
            then(mul(c_("wi"), c_("t2"), c_("inv")))
            for lo, hi, base in ((2, 3, 1), (3, 5, 2), (5, 9, 4)):
                n = hi - lo
                k = (P, n, Q)
                cmul(pw_re[:, lo:hi], pw_im[:, lo:hi], (pw_re[:, lo - base:hi - base], pw_im[:, lo - base:hi - base]),
                     (pw_re[:, base:base + 1].to_broadcast(k), pw_im[:, base:base + 1].to_broadcast(k)), pwrev[:, 0, 0:n])
            for m in range(J):
                mark(vv.tensor_copy(pwrev[:, 0, m], pw_re[:, J - 1 - m]))
                mark(vv.tensor_copy(pwrev[:, 1, m], pw_im[:, J - 1 - m]))
            sc = (P, Q, CH)
            tsmall = ctmp[:, 0:Q * CH].rearrange("p (q c) -> p q c", q=Q)
            cmul(b_bar[0], b_bar[1], b_raw, (c_("wr").unsqueeze(2).to_broadcast(sc), c_("wi").unsqueeze(2).to_broadcast(sc)), tsmall)
            sh = (P, Q, J, CH)
            tb = ctmp[:, 0:Q * J * CH].rearrange("p (q j c) -> p q j c", q=Q, j=J)
            cmul(bt_pre[0], bt_pre[1], [b.unsqueeze(2).to_broadcast(sh) for b in b_bar],
                 [pwrev[:, r].rearrange("p j q -> p q j").unsqueeze(3).to_broadcast(sh) for r in range(2)], tb)
            vv.tensor_copy(stat[:, 61:62], stat[:, 28:29]).then_inc(btpre_ready, 1)
            taken(v, "ct")
            sh = (P, Q, J + 1, CH)
            tc_ = ctmp.rearrange("p (q j c) -> p q j c", q=Q, j=J + 1)
            cmul(cp_re, cp_im, [c.unsqueeze(2).to_broadcast(sh) for c in c_T],
                 [w.rearrange("p j q -> p q j").unsqueeze(3).to_broadcast(sh) for w in (pw_re[:], pw_im[:])], tc_, neg_im=True)
            vv.tensor_copy(stat[:, 61:62], stat[:, 28:29]).then_inc(cp_ready, 1)
            ph = [(c_("cos"), c_("sin")), (c_("cr1"), c_("ci1")), (c_("cr2"), c_("ci2"))]
            src = 0
            for n in range(3):
                dst = 1 if src != 1 else 2
                cmul(*ph[dst], ph[src], ph[src], c_("t1"))
                src = dst
            mark(vv.memset(tab_c[:, :, 0:1], 1.0))
            then(vv.memset(tab_s[:, :, 0:1], 0.0))
            tt = st.rearrange("p (q c) -> p q c", q=2 * Q)[:, 0:Q]
            n = 1
            while n < NC:
                k = (P, Q, n)
                cmul(tab_c[:, :, n:2 * n], tab_s[:, :, n:2 * n], (tab_c[:, :, 0:n], tab_s[:, :, 0:n]),
                     [z.unsqueeze(2).to_broadcast(k) for z in ph[src]], tt[:, :, 0:n])
                n *= 2
                if n < NC:
                    dst = 1 if src != 1 else 2
                    cmul(*ph[dst], ph[src], ph[src], c_("t1"))
                    src = dst

            for i in range(NT):
                taken(v, ("v", i))
                then(vv.bn_stats(stat[:, 44:50], V[:, i]))
                mark(vv.bn_aggr(mean_var[:, 2 * i:2 * i + 2], stat[:, 44:50]))
                step.wait()
            v.wait_ge(consts_in, 16 * 12)
            vv.tensor_copy(stat[:, 32:36], mean_var[:].rearrange("p (i two) -> p two i", two=2)[:, 1]).then_inc(var_ready, 1)
            v.wait_ge(vstd_ready, 1)
            then(vv.reciprocal(stat[:, 36:40], stat[:, 40:44]))
            for i in range(NT):
                then(vv.tensor_scalar(V[:, i], V[:, i], mean_var[:, 2 * i:2 * i + 1], stat[:, 36 + i:37 + i], ALU.subtract, ALU.mult))
                then(mul(V[:, i], V[:, i], lng[:]))
                add(V[:, i], V[:, i], lnb[:]).then_inc(vn_ready, 1)

            v.wait_ge(diff_ready, MW)
            for h in range(2):
                qs = slice(8 * h, 8 * h + 8)
                b_re = full(v, ("bu", h, 0)).rearrange("p (q c) -> p q c", q=8)
                b_im = full(v, ("bu", h, 1)).rearrange("p (q c) -> p q c", q=8)
                mark(mul(rot[0], b_re, tab_c[:, qs]))
                mark(mul(rot[1], b_im, tab_s[:, qs]))
                then(mul(rot[2], b_re, tab_s[:, qs]))
                vv.tensor_tensor(st_re[:, qs], rot[0], rot[1], ALU.add).then_inc(out_of(("bu", h, 0)), 1)
                taken(v, ("bu", h, 0))
                then(mul(rot[0], b_im, tab_c[:, qs]))
                vv.tensor_tensor(st_im[:, qs], rot[0], rot[2], ALU.subtract).then_inc(out_of(("bu", h, 1)), 1)
                taken(v, ("bu", h, 1))
            for q in range(Q):
                decay = c_("rho")[:, q:q + 1].to_broadcast((P, NC))
                for z in (st_re, st_im):
                    mark(vv.tensor_tensor_scan(z[:, q], decay, z[:, q], 0.0, ALU.mult, ALU.add))
            step.wait()
            for h in range(2):
                qs, c0 = slice(8 * h, 8 * h + 8), slice(0, NC - 1)
                r0, r1, r2 = (r[:, :, c0] for r in rot)
                mark(mul(r0, st_re[:, qs, c0], tab_c[:, qs, c0]))
                mark(mul(r1, st_im[:, qs, c0], tab_s[:, qs, c0]))
                then(mul(r2, st_re[:, qs, c0], tab_s[:, qs, c0]))
                then(sub(st_re[:, qs, 1:NC], r0, r1))
                then(mul(r0, st_im[:, qs, c0], tab_c[:, qs, c0]))
                then(add(st_im[:, qs, 1:NC], r2, r0))
            then(vv.memset(st_re[:, :, 0:1], 0.0))
            vv.memset(st_im[:, :, 0:1], 0.0).then_inc(st_ready, 1)

            taken(v, ("u", MW - 1))
            for h in range(4):
                name = ("sg", h)
                vv.tensor_tensor(U[:, h], U[:, h], full(v, name), ALU.mult).then_inc(out_of(name), 1)

            def merge(n):
                half, k_ = GATE_STEPS[n]
                for m in range(MW):
                    i = n * MW + m
                    name = ("br", n, m)
                    taken(v, ("gt", n, m))
                    bank, dst = full(v, name), M[:, half * MW + m]
                    if k_ == 0:
                        ins = vv.tensor_tensor(dst, sig[i % 2], bank, ALU.mult)
                        ins.then_inc(out_of(name), 1)
                        taken(v, name)
                    else:
                        vv.tensor_tensor(prod, sig[i % 2], bank, ALU.mult).then_inc(merge_mul, 1)
                        muls[0] += 1
                        v.wait_ge(merge_mul, muls[0])
                        vv.tensor_tensor(dst, dst, prod, ALU.add).then_inc(out_of(name), 1)
                        taken(v, name)
                    vv.tensor_copy(stat[:, 61:62], stat[:, 28:29]).then_inc(merge_done, 1)

            muls = [0]
            v.wait_ge(ker_in, 16 * J)
            merge(0)
            v.wait_ge(yT_in, 16)
            for m in range(MW):
                vv.scalar_tensor_tensor(yT[:, m], C[:, m], cols[:, DSK + m:DSK + m + 1], yT[:, m], ALU.mult, ALU.add).then_inc(ych_ready, 1)
            merge(1)
            for m in range(MW):
                taken(v, ("gl", m))
            for m in range(MW):
                vv.tensor_tensor(C[:, m], C[:, m], yT[:, m], ALU.mult).then_inc(yc_ready, 1)
            for n in range(2, 6):
                merge(n)

            v.wait_ge(x_again, 16)

            def residual(i):
                for h in range(2):
                    name = ("o", i, h)
                    dst = x3[:, i, W * h:W * (h + 1)]
                    vv.tensor_tensor(dst, dst, full(v, name), ALU.add).then_inc(out_of(name), 1)

            def normed(i):
                v.wait_ge(std2_ready, i + 1)
                then(vv.reciprocal(stat[:, 50 + i:51 + i], stat[:, 12 + i:13 + i]))
                if i >= 2:
                    v.wait_ge(h2_stored[i % 2], 16)
                    full(v, ("rt", i - 2, 1))
                vv.tensor_scalar(h2n[i % 2], x3[:, i], stat[:, 50 + i:51 + i], None, ALU.mult).then_inc(h2_ready, 1)

            def routed(i):
                for h in range(2):
                    name = ("rt", i, h)
                    vv.tensor_tensor(h2T[:, 4 * h:4 * h + 4], full(v, name).rearrange("p (k t) -> p k t", k=4),
                                     cols[:, GFF + 4 * h:GFF + 4 * h + 4].unsqueeze(2).to_broadcast((P, 4, P)),
                                     ALU.mult).then_inc(out_of(name), 1)
                name = ("lg", i)
                vv.tensor_copy(logits_zone[:, i], full(v, name)[:, 0:36]).then_inc(out_of(name), 1)

            for i in range(NT):
                residual(i)
                if i >= 1:
                    routed(i - 1)
                normed(i)
            routed(NT - 1)
            for i in range(NT):
                taken(v, ("lg", i))

            L4 = logits_zone[:, :, 0:4]
            L32 = logits_zone[:, :, 4:36].rearrange("p i (g e) -> p i g e", g=4)

            def first_max(vals, best, cand, low, onehot, width):
                sh = (P, NT, width)
                then(vv.tensor_reduce(best, vals, X, ALU.max))
                then(vv.tensor_tensor(onehot, vals, best.to_broadcast(sh), ALU.is_equal))
                then(vv.scalar_tensor_tensor(cand, onehot, -100.0, iot[:, 0:width].unsqueeze(1).to_broadcast(sh), ALU.mult, ALU.add))
                then(vv.tensor_reduce(low, cand, X, ALU.min))
                then(vv.tensor_tensor(onehot, cand, low.to_broadcast(sh), ALU.is_equal))

            first_max(L4, R["gmax"], R["cand"], R["cmin"], R["ohg"], 4)
            vv.tensor_tensor(R["dg"], L4, R["gmax"].to_broadcast((P, NT, 4)), ALU.subtract).then_inc(exp_in, 1)
            s4 = (P, NT, 4, GE)
            then(mul(R["sel"], L32, R["ohg"].unsqueeze(3).to_broadcast(s4)))
            then(vv.tensor_reduce(R["esel"], R["sel"].rearrange("p i g e -> p i e g"), X, ALU.add))
            first_max(R["esel"], R["m1"], R["cand8"], R["min8"], R["oh1"], GE)
            then(axpy(R["e2"], R["oh1"], -BIG, R["esel"]))
            first_max(R["e2"], R["m2"], R["cand8"], R["min8"], R["oh2"], GE)
            vv.tensor_tensor(R["dm"], R["m2"], R["m1"], ALU.subtract).then_inc(exp2_in, 1)
            for M_, o_ in (("M1", "oh1"), ("M2", "oh2")):
                mark(mul(R[M_], R["ohg"].unsqueeze(3).to_broadcast(s4), R[o_].unsqueeze(2).to_broadcast(s4)))
            step.wait()
            M1, M2 = (R[m].rearrange("p i g e -> p i (g e)") for m in ("M1", "M2"))
            add(oh, M1, M2).then_inc(onehot_ready, 1)
            v.wait_ge(exp_out, 1)
            then(vv.tensor_reduce(R["gsum"], R["ex4"], X, ALU.add))
            then(vv.reciprocal(R["gp"], R["gsum"]))
            v.wait_ge(exp2_out, 1)
            then(vv.tensor_scalar(R["den"], R["ex"], 1.0, None, ALU.add))
            then(vv.reciprocal(R["den"], R["den"]))
            w1, w2 = (wts[:, NT * c:NT * (c + 1)].unsqueeze(2) for c in range(2))
            then(mul(w1, R["den"], R["gp"]))
            then(mul(w2, w1, R["ex"]))
            mark(vv.tensor_scalar(R["e64"], iot[:, 0:NE], float(CAP), None, ALU.mult))
            bank = full(v, "pos")
            then(vv.tensor_copy(R["cnt"], bank[:, NE * NT:NE * (NT + 1)]))
            then(vv.tensor_scalar(R["ov"], R["cnt"], float(CAP), None, ALU.is_gt))
            for k in range(2, T // CAP):
                then(vv.scalar_tensor_tensor(R["ov"], R["cnt"], float(CAP * k), R["ov"], ALU.is_gt, ALU.add))
            then(vv.tensor_tensor_scan(R["incl"], lnb[:, 0:NE], R["ov"], 0.0, ALU.mult, ALU.add))
            then(sub(R["base"], R["incl"], R["ov"]))
            then(axpy(R["base"], R["base"], float(CAP), R["e64"], ALU.subtract))
            then(vv.tensor_scalar(R["base"], R["base"], float(NE * CAP - CAP), None, ALU.add))
            se = (P, NT, NE)
            vv.tensor_copy(R["pos"], bank[:, 0:NE * NT].rearrange("p (i e) -> p i e", i=NT)).then_inc(out_of("pos"), 1)
            taken(v, "pos")
            then(vv.tensor_scalar(R["row"], R["pos"], float(CAP), None, ALU.is_ge))
            then(mul(R["row"], R["row"], R["base"].unsqueeze(1).to_broadcast(se)))
            then(add(R["row"], R["row"], R["pos"]))
            then(add(R["row"], R["row"], R["e64"].unsqueeze(1).to_broadcast(se)))
            for c, m in enumerate((M1, M2)):
                then(mul(R["pick"], R["row"], m))
                then(vv.tensor_reduce(R["rowf"][:, c:c + 1].rearrange("p a i -> p i a"), R["pick"], X, ALU.add))
            vv.tensor_copy(row_u[:], R["rowf"].rearrange("p c i -> p (c i)")).then_inc(rows_ready, 1)
            so = (1, NOV, NE)
            then(vv.tensor_tensor(R["le"][0:1], R["incl"][0:1].unsqueeze(1).to_broadcast(so),
                                  iot[0:1, 0:NOV].unsqueeze(2).to_broadcast(so), ALU.is_le))
            then(vv.tensor_reduce(R["eid"][0:1].unsqueeze(2), R["le"][0:1], X, ALU.add))
            then(vv.tensor_scalar(ovi[0:1, 0:NOV], R["eid"][0:1], float(NE - 1), None, ALU.min))
            vv.tensor_copy(ovi[0:1, NOV:NOV + 1], R["incl"][0:1, NE - 1:NE]).then_inc(ov_ready, 1)
            vv.tensor_copy(idx_u[:], full(v, "tok")[0:CAP, 0:NB]).then_inc(out_of("tok"), 1)
            taken(v, "tok")
            vv.tensor_copy(stat[:, 61:62], stat[:, 28:29]).then_inc(idx_ready, 1)
            experts_vector(v)

        @block.gpsimd
        def _(gp):
            g = nc.gpsimd
            step = Steps(gp, gp_step)
            then, mark = step.then, step.mark
            then(g.memset(ident[:], 0.0))
            g.affine_select(out=ident[:], in_=ident[:], compare_op=ALU.not_equal, fill=1.0, base=0,
                            pattern=[[-1, P]], channel_multiplier=1).then_inc(ident_ready, 1)
            gp.wait_ge(params_in, 16 * 8)
            g.tensor_copy(par_nat[:, 2].rearrange("q (two p) -> q two p", two=2),
                          ldt_nat.unsqueeze(2).to_broadcast((Q, 2, S))).then_inc(ldt_spread, 1)
            g.affine_select(out=sgw_nat, in_=sgw_nat, compare_op=ALU.is_ge, fill=0.0, base=0,
                            pattern=[[0, 4], [-1, P]], channel_multiplier=1).then_inc(sgw_masked, 1)
            mark(g.memset(ones_row[:], 1.0))
            for i in range(16):
                mark(g.memset(icnt[:, i:i + 1], 1.0 / (i + 1)))
            mark(g.iota(iot_i[:, 0:48], pattern=[[1, 48]], base=0, channel_multiplier=0))
            then(g.iota(iot_i[:, 48:52], pattern=[[P, NT]], base=0, channel_multiplier=1))
            then(g.tensor_copy(iot[:], iot_i[:]))
            for w_ in win:
                mark(g.memset(w_[:, 0:PAD], 0.0))
            then(g.memset(zeros[:], 0.0))
            g.memset(eps, EPS).then_inc(consts_made, 1)
            gp.dma_start(tok_d.rearrange("(n c) a -> n (c a)", n=NB), zeros[:]).then_inc(tok_zero, 16)
            full(gp, ("x", NT - 1, 1))
            g.memset(xb[:], 0.0).then_inc(toep_zero, 1)
            for m in range(MW):
                taken(gp, ("a", m))
                src, wide = A[:, m], 2 ** (m + 1)
                cur = 0
                then(g.tensor_copy(win[0][:, PAD:], src))
                for k in range(m + 1):
                    s_ = 2 ** k
                    then(g.tensor_tensor(win[1 - cur][:, PAD:], win[cur][:, PAD:], win[cur][:, PAD - s_:PAD + T - s_], ALU.add))
                    cur = 1 - cur
                w_ = win[cur]
                mark(g.tensor_tensor(w_[:, PAD:PAD + wide], w_[:, PAD:PAD + wide], icnt[:, 0:wide], ALU.mult))
                then(g.tensor_scalar(w_[:, PAD + wide:], w_[:, PAD + wide:], 1.0 / wide, None, ALU.mult))
                g.tensor_tensor(src, w_[:, PAD:], src, ALU.subtract).then_inc(diff_ready, 1)
                gp.wait_ge(diff_ready, m + 1)
            gp.wait_ge(vn_ready, NT)
            mark(g.memset(lnb[:, 0:P], 1.0))
            then(g.memset(lng[:, 0:P], 1.0))
            g.affine_select(out=lng[:, 0:P], in_=lng[:, 0:P], compare_op=ALU.is_gt, fill=0.0, base=0,
                            pattern=[[1, P]], channel_multiplier=-1).then_inc(masks_ready, 1)
            for i in range(NT):
                gp.wait_ge(h2_ready, i + 1)
                gp.dma_start(h2_d[i * P:(i + 1) * P, :], h2n[i % 2]).then_inc(h2_stored[i % 2], 16)
            gp.wait_ge(tok_zero, 16)
            gp.wait_ge(rows_ready, 1)
            for c in range(2):
                for i in range(NT):
                    j = NT * c + i
                    g.indirect_dma_start(tok_d, bass.IndirectOffsetOnAxis(ap=row_u[:, j:j + 1], axis=0),
                                         iot[:, 48 + i:49 + i], None).then_inc(tok_scattered, 16)
            gp.wait_ge(tok_scattered, 16 * 2 * NT)
            gp.dma_start(tok_rows, tok_d.rearrange("(n c) a -> n (c a)", n=NB)).then_inc(tok_in, 16)
            experts_gpsimd(gp)


INPUTS = ["x", "norm_mix_g", "w_in", "b_gate", "pool_w", "pool_scale", "sgu_ln_g", "sgu_ln_b", "sgu_w", "sgu_b",
          "ssm_a_re", "ssm_a_im", "ssm_log_dt", "ssm_b_re", "ssm_b_im", "ssm_c_re", "ssm_c_im", "ssm_d", "glu_w",
          "glu_b", "w_branch", "w_out", "norm_ffn_g", "router_group_w", "router_group_b", "router_expert_w",
          "router_expert_b", "exp_w_gate", "exp_w_up", "exp_w_down", "norm_final_g"]


def kernel(**inputs):
    import concourse.bacc as bacc
    from concourse.bass_utils import run_bass_kernel_spmd

    nc = bacc.Bacc("TRN2", target_bir_lowering=False, num_devices=1)
    arrays, args = {}, []
    for name in INPUTS:
        a = np.ascontiguousarray(inputs[name])
        arrays[f"in_{name}"] = a
        args.append(nc.dram_tensor(f"in_{name}", a.shape, mybir.dt.from_np(a.dtype), kind="ExternalInput").ap())
    args.append(nc.dram_tensor("out", (1, T, D), F32, kind="ExternalOutput").ap())
    trunk(nc, *args)
    r = run_bass_kernel_spmd(nc, [arrays], core_ids=[0])
    return r.results[0]["out"]
```

```python
from contextlib import ExitStack
import math

import numpy as np
import concourse.bass as bass
from concourse import mybir

F32 = mybir.dt.float32
F32R = mybir.dt.float32r
I32 = mybir.dt.int32
U32 = mybir.dt.uint32
ALU = mybir.AluOpType
ACT = mybir.ActivationFunctionType
X = mybir.AxisListType.X

P = 128
T = 512
NT = T // P
D = 1024
KD = D // P
W = 512
MW = W // P
EPS = 1e-6

G = 32
Q = G // 2
S = 64
CH = 16
J = 8
NC = T // J

NE = 32
F = 512
KF = F // P
CAP = 64
NOV = 2 * T // CAP - 2
NB = 2 * NE + NOV
BIG = 3.0e38
MAGIC = 12582912.0

C_SSM, C_V, C_POOL, C_U = 1536, 1024, 0, 512
GATE_STEPS = [(half, k) for k in range(3) for half in range(2)]
WIN_COLS = [C_SSM, C_POOL, C_U, C_V] + [2048 + k * D + half * W for half, k in GATE_STEPS]

PRM = ["are", "aim", "ldt", "dt", "r", "th", "n", "n2", "t1", "t2", "t3", "thr", "nhalf", "s", "c", "cosm1",
       "cos", "sin", "e1", "rho", "tanh", "one_m", "inv", "em1", "nr", "ni", "m2", "wr", "wi",
       "cr1", "ci1", "cr2", "ci2", "ab"]



def psum_groups():
    g = ["par", "ct", "wst"]
    g += [("x", i, h) for i in range(NT) for h in range(2)]
    g += [("c", m) for m in range(MW)] + [("a", m) for m in range(MW)]
    g += [("bt", r, i) for r in range(2) for i in range(4)] + [("k", i) for i in range(8)]
    g += [("bu", h, r) for h in range(2) for r in range(2)] + [("u", m) for m in range(MW)]
    g += [("y", i) for i in range(4)] + [("v", i) for i in range(NT)] + [("gl", m) for m in range(MW)]
    g += [("py", m) for m in range(MW)] + [("sg", h) for h in range(4)]
    for n in range(len(GATE_STEPS)):
        g += [f for m in range(MW) for f in (("gt", n, m), ("br", n, m))]
    for i in range(NT):
        g += [("o", i, 0), ("o", i, 1)]
        if i >= 1:
            g += [("rt", i - 1, 0), ("rt", i - 1, 1), ("lg", i - 1)]
    g += [("rt", NT - 1, 0), ("rt", NT - 1, 1), ("lg", NT - 1), "pos", "tok"]
    return {name: (i % 8, i // 8 + 1) for i, name in enumerate(g)}


class Steps:

    def __init__(self, eng, sem):
        self.eng, self.sem, self.n = eng, sem, 0

    def mark(self, ins):
        self.n += 1
        ins.then_inc(self.sem, 1)

    def wait(self):
        self.eng.wait_ge(self.sem, self.n)

    def then(self, ins):
        self.mark(ins)
        self.wait()


def trunk(nc, x, norm_mix_g, w_in, b_gate, pool_w, pool_scale, sgu_ln_g, sgu_ln_b, sgu_w, sgu_b,
          ssm_a_re, ssm_a_im, ssm_log_dt, ssm_b_re, ssm_b_im, ssm_c_re, ssm_c_im, ssm_d, glu_w, glu_b,
          w_branch, w_out, norm_ffn_g, router_group_w, router_group_b, router_expert_w, router_expert_b,
          exp_w_gate, exp_w_up, exp_w_down, norm_final_g, out):
    place = psum_groups()

    xc_d = nc.dram_tensor("xc_scratch", (W, T), F32, kind="Internal").ap()
    y_d = nc.dram_tensor("y_scratch", (W, T), F32, kind="Internal").ap()
    h2_d = nc.dram_tensor("h2_scratch", (T, D), F32, kind="Internal").ap()
    tok_d = nc.dram_tensor("token_of_slot", (NB * CAP, 1), F32, kind="Internal").ap()
    res_d = nc.dram_tensor("result_rows", (NB * CAP, D), F32, kind="Internal").ap()

    with ExitStack() as ctx:
        ctx.enter_context(nc.allow_non_contiguous_dma(reason="small parameter vectors"))

        def sb(name, shape, dt=F32):
            return ctx.enter_context(nc.sbuf_tensor(name, shape, dt))

        def sem(name):
            return ctx.enter_context(nc.semaphore(name))

        ps = ctx.enter_context(nc.psum_tensor("ps", [P, 8, 512], F32))

        base = (nc.sbuf_base + 31) // 32 * 32
        ring = sb("ring", [P, 6, 4096])
        xb = sb("xb", [P, 4096])
        hb = sb("hb", [P, 4096])
        ab = sb("ab", [P, 2048])
        ub = sb("ub", [P, 2048])
        cb = sb("cb", [P, 2048])
        vb = sb("vb", [P, 2048])
        mb = sb("mb", [P, 4096])
        late = sb("late", [P, 2048])
        lng = late[:, 0:W]
        lnb = late[:, W:2 * W]
        wst = late[:, 2 * W:3 * W].rearrange("p (h t) -> p h t", h=4)
        poolw = late[:, 3 * W:4 * W].rearrange("p (g d) -> p g d", g=4)
        ident = sb("ident", [P, P])

        def overlaid(name, shape, floats):
            return nc.alloc_sbuf_tensor_at(name, shape, F32R, offset=base + 4 * floats)

        O_X, O_H, O_A, O_U, O_C = (4096 * 6 + d for d in (0, 4096, 8192, 10240, 12288))
        O_LATE = 4096 * 6 + 8192 + 4 * 2048 + 4096
        h_hi, h_lo = overlaid("h_hi", [P, KD, T], O_X), overlaid("h_lo", [P, KD, T], O_H)
        y_hi = overlaid("y_hi", [P, MW, T], O_LATE)
        y_lo = [overlaid(f"y_lo{k}", [P, MW, T], at) for k, at in enumerate((O_A, O_U, O_C))]
        SW = W // 2
        wg_hi, wg_lo, wb_hi, wb_lo = ([overlaid(f"{n}{s}", [P, k, SW], 4096 * 2 + 6144 * s + at) for s in range(2)]
                                      for n, k, at in (("wg_hi", KD, 0), ("wg_lo", KD, 2048), ("wb_hi", MW, 4096), ("wb_lo", MW, 5120)))
        prm = sb("prm", [P, len(PRM), Q])
        pw_re = sb("pw_re", [P, J + 1, Q])
        pw_im = sb("pw_im", [P, J + 1, Q])
        pwrev = sb("pwrev", [P, 2, J, Q])
        icnt = sb("icnt", [P, 16])
        cols = sb("cols", [P, 64])
        stat = sb("stat", [P, 64])
        mean_var = sb("mean_var", [P, 2 * NT])
        bs_row = sb("bs_row", [1, 4, P])
        ones_row = sb("ones_row", [1, P])
        rbias = sb("rbias", [1, 36])
        iot_i = sb("iot_i", [P, 52], I32)
        iot = sb("iot", [P, 52])
        zeros = sb("zeros", [NB, CAP])
        idx_u = sb("idx_u", [CAP, NB], U32)
        idx_now = sb("idx_now", [CAP, 4], U32)
        row_u = sb("row_u", [P, 8], U32)
        wts = sb("wts", [P, 8])
        ovi = sb("ovi", [1, NOV + 1], I32)
        second = sb("second", [1, 2, NE], I32)

        BG, GB, PSC, DSK, GMX, GFF, GFX = 0, 24, 28, 32, 36, 44, 52
        x3 = xb[:].rearrange("p (i d) -> p i d", i=NT)
        toep = xb[:].rearrange("p (g n) -> p g n", g=G)
        hT = hb[:].rearrange("p (k t) -> p k t", k=KD)
        A = ab[:].rearrange("p (m t) -> p m t", m=MW)
        U = ub[:].rearrange("p (m t) -> p m t", m=MW)
        C = cb[:].rearrange("p (m t) -> p m t", m=MW)
        V = vb[:].rearrange("p (m t) -> p m t", m=MW)
        M = mb[:].rearrange("p (k t) -> p k t", k=KD)
        slot_k = [ring[:, s].rearrange("p (k n) -> p k n", k=KD) for s in range(6)]
        slot_h = [ring[:, s].rearrange("p (k n) -> p k n", k=KF) for s in range(6)]

        spare = ring[:, 2:5].rearrange("p s n -> p (s n)")
        NCP = Q * (J + 1) * CH
        cp_re = spare[:, 0:NCP].rearrange("p (q j c) -> p q j c", q=Q, j=J + 1)
        cp_im = spare[:, NCP:2 * NCP].rearrange("p (q j c) -> p q j c", q=Q, j=J + 1)
        o = 2 * NCP
        u8 = spare[:, o:o + 2048]
        y8 = spare[:, o + 2048:o + 4096]
        st = spare[:, o + 4096:o + 6144]
        tmp6 = spare[:, o + 6144:o + 7680]
        assert o + 7680 == 3 * 4096
        ctmp = spare[:, o + 2048:o + 2048 + NCP]
        btT = [ring[:, 5, Q * P * r:Q * P * (r + 1)].rearrange("p (q n) -> p q n", q=Q) for r in range(2)]
        u8v = u8.rearrange("p (g c) -> p g c", g=G)
        y8v = y8.rearrange("p (g c) -> p g c", g=G)
        yT = u8.rearrange("p (m t) -> p m t", m=MW)
        st_re = st[:, 0:Q * NC].rearrange("p (q c) -> p q c", q=Q)
        st_im = st[:, Q * NC:2 * Q * NC].rearrange("p (q c) -> p q c", q=Q)
        tab_c = y8[:, 0:Q * NC].rearrange("p (q c) -> p q c", q=Q)
        tab_s = y8[:, Q * NC:2 * Q * NC].rearrange("p (q c) -> p q c", q=Q)
        rot = [tmp6[:, 512 * i:512 * (i + 1)].rearrange("p (q c) -> p q c", q=Q // 2) for i in range(3)]
        PAD = 16
        win = [tmp6[:, (PAD + T) * i:(PAD + T) * (i + 1)] for i in range(2)]
        bt_pre = [mb[:, Q * P * r:Q * P * (r + 1)].rearrange("p (q j c) -> p q j c", q=Q, j=J) for r in range(2)]
        ker = mb[0:CH].rearrange("p (g n) -> p g n", g=G)
        gluw = mb[:, 2048:4096].rearrange("p (k n) -> p k n", k=MW)
        b_raw = [ub[:, 256 * r:256 * (r + 1)].rearrange("p (q c) -> p q c", q=Q) for r in range(2)]
        b_bar = [ub[:, 512 + 256 * r:768 + 256 * r].rearrange("p (q c) -> p q c", q=Q) for r in range(2)]
        c_T = [ub[:, 1024 + 256 * r:1280 + 256 * r].rearrange("p (q c) -> p q c", q=Q) for r in range(2)]
        c_nat = [ub[:, 1536 + 256 * r:1792 + 256 * r].rearrange("p (t n) -> p t n", t=2) for r in range(2)]
        sgw_nat = vb[:, 0:512].rearrange("p (h s) -> p h s", h=4)
        par_nat = vb[0:Q, 512:512 + 3 * P].rearrange("q (n p) -> q n p", n=3)
        ldt_nat = vb[0:Q, 1024:1026]

        wb_slot = [ring[:, 5, 2048 * i:2048 * (i + 1)].rearrange("p (k n) -> p k n", k=MW) for i in range(2)]
        rw = vb[:, 0:KD * 36].rearrange("p (k n) -> p k n", k=KD)
        sig = [vb[:, 512 + 512 * i:1024 + 512 * i] for i in range(2)]
        prod = vb[:, 1536:2048]
        h2n = [hb[:, 1024 * i:1024 * (i + 1)] for i in range(2)]
        h2T = hb[:, 2048:3072].rearrange("p (k t) -> p k t", k=KD)
        tok_rows = hb[0:NB, 4032:4096]

        xg = [ab[0:CAP, 1024 * b:1024 * (b + 1)] for b in range(2)]
        xgT = [ub[:, 512 * b:512 * (b + 1)].rearrange("p (k t) -> p k t", k=KD) for b in range(2)]
        silu = [ub[:, 1024 + 256 * b:1280 + 256 * b] for b in range(2)]
        act_ = [ub[:, 1536 + 256 * b:1792 + 256 * b] for b in range(2)]
        actT = [cb[:, 256 * b:256 * (b + 1)].rearrange("p (j n) -> p j n", j=2) for b in range(2)]
        res = [cb[:, 512 + 512 * b:1024 + 512 * b] for b in range(2)]

        eps = stat[:, 60:61]
        zones = [[vb, 512, 2048], [hb, 3072, 4032]]

        def table(*shape):
            n = int(np.prod(shape))
            z = next(z for z in zones if z[1] + n <= z[2])
            z[1] += n
            a = z[0][:, z[1] - n:z[1]]
            if len(shape) == 2:
                a = a.rearrange("p (a b) -> p a b", a=shape[0])
            if len(shape) == 3:
                a = a.rearrange("p (a b c) -> p a b c", a=shape[0], b=shape[1])
            return a

        GE = NE // 4
        logits_zone = hb[:, 3072:3072 + NT * 36].rearrange("p (i n) -> p i n", i=NT)
        zones[1][1] += NT * 36
        R = {name: table(*shape) for name, shape in {
            "gmax": (NT, 1), "dg": (NT, 4), "cand": (NT, 4), "cmin": (NT, 1), "ohg": (NT, 4), "ex4": (NT, 4),
            "gsum": (NT, 1), "gp": (NT, 1), "sel": (NT, 4, GE), "esel": (NT, GE), "m1": (NT, 1), "cand8": (NT, GE),
            "min8": (NT, 1), "oh1": (NT, GE), "e2": (NT, GE), "m2": (NT, 1), "oh2": (NT, GE), "dm": (NT, 1),
            "ex": (NT, 1), "den": (NT, 1), "M1": (NT, 4, GE), "M2": (NT, 4, GE), "oh": (NT, NE), "pos": (NT, NE),
            "row": (NT, NE), "pick": (NT, NE), "cnt": (NE,), "ov": (NE,), "incl": (NE,), "base": (NE,),
            "has2": (NE,), "cum2": (NE,), "ord2": (NE,), "e64": (NE,), "rowf": (2, NT), "le": (NOV, NE), "eid": (NOV,)}.items()}
        oh = R["oh"]

        def c_(name):
            return prm[:, PRM.index(name)]

        x_in = [sem(f"x_in{i}") for i in range(NT)]
        params_in, consts_in, b_in = sem("params_in"), sem("consts_in"), sem("b_in")
        win_in = [sem(f"win_in{s}") for s in range(2)]
        wb_in = [sem(f"wb_in{s}") for s in range(2)]
        glu_in, router_in = sem("glu_in"), sem("router_in")
        x_again = sem("x_again")
        xc_stored, u8_in, y_stored, yT_in, ker_in = (sem(n) for n in ("xc_stored", "u8_in", "y_stored", "yT_in", "ker_in"))
        bank_full = [sem(f"bank_full{b}") for b in range(8)]
        bank_out = [sem(f"bank_out{b}") for b in range(8)]
        ident_ready, sgw_masked, ldt_spread, consts_made = (sem(n) for n in ("ident_ready", "sgw_masked", "ldt_spread", "consts_made"))
        gp_step, dve_step = sem("gp_step"), sem("dve_step")
        ssq_ready, std_ready, xn_ready = sem("ssq_ready"), sem("std_ready"), sem("xn_ready")
        dt_ready, angle_ready, act_prm = sem("dt_ready"), sem("angle_ready"), sem("act_prm")
        cp_ready, btpre_ready = sem("cp_ready"), sem("btpre_ready")
        var_ready, vstd_ready, vn_ready = sem("var_ready"), sem("vstd_ready"), sem("vn_ready")
        toep_zero, diff_ready, st_ready = sem("toep_zero"), sem("diff_ready"), sem("st_ready")
        ych_ready, yg_ready, yc_ready = sem("ych_ready"), sem("yg_ready"), sem("yc_ready")
        h_hi_ready, h_lo_ready, w_hi_ready, w_lo_ready, y_hi_ready, y_lo_ready = (
            sem(n) for n in ("h_hi_ready", "h_lo_ready", "w_hi_ready", "w_lo_ready", "y_hi_ready", "y_lo_ready"))
        merge_mul, merge_done, masks_ready = sem("merge_mul"), sem("merge_done"), sem("masks_ready")
        ssq2_ready, std2_ready, h2_ready = sem("ssq2_ready"), sem("std2_ready"), sem("h2_ready")
        h2_stored = [sem(f"h2_stored{i}") for i in range(2)]
        onehot_ready, exp_in, exp_out, exp2_in, exp2_out = (sem(n) for n in ("onehot_ready", "exp_in", "exp_out", "exp2_in", "exp2_out"))
        tok_zero, rows_ready, tok_scattered, tok_in = sem("tok_zero"), sem("rows_ready"), sem("tok_scattered"), sem("tok_in")
        out_stored, gfin_in, sums_ready, ssq3_ready, std3_ready, outrow_ready = (
            sem(n) for n in ("out_stored", "gfin_in", "sums_ready", "ssq3_ready", "std3_ready", "outrow_ready"))
        over_zero = sem("over_zero")
        fin_step = sem("fin_step")
        passed = sem("passed")
        picked = [sem(f"picked{i}") for i in range(NT)]
        idx_ready, ov_ready, idx_copied, ov_idx_copied = (sem(n) for n in ("idx_ready", "ov_ready", "idx_copied", "ov_idx_copied"))
        KINDS = ("gate", "up", "down")

        def per_side(name):
            return [sem(f"{name}{b}") for b in range(2)]

        ew_in = [{k: sem(f"{k}_weights_in{b}") for k in KINDS} for b in range(2)]
        done = [{k: sem(f"{k}_done{b}") for k in KINDS} for b in range(2)]
        xg_in, xt_full, xgT_ready, silu_ready = per_side("xg_in"), per_side("xt_full"), per_side("xgT_ready"), per_side("silu_ready")
        act_ready, at_full, actT_ready = per_side("act_ready"), per_side("at_full"), per_side("actT_ready")
        res_ready, res_stored = per_side("res_ready"), per_side("res_stored")
        done2 = {k: sem(f"second_{k}_done") for k in KINDS}
        (xg2_in, xt2_full, xgT2_ready, silu2_ready, act2_ready, at2_full, actT2_ready, res2_ready, res2_stored,
         idx2_copied, results_stored) = (
            sem("second_" + n) for n in ("xg_in", "xt_full", "xgT_ready", "silu_ready", "act_ready", "at_full",
                                         "actT_ready", "res_ready", "res_stored", "idx_copied",
                                         "results_stored"))
        ov_w, ov_done = sem("ov_weights_in"), {k: sem(f"ov_{k}_done") for k in KINDS}
        (ov_xg_in, ov_xt_full, ov_xgT_ready, ov_silu_ready, ov_act_ready, ov_at_full, ov_actT_ready, ov_res_ready,
         ov_res_stored) = (sem("ov_" + n) for n in ("xg_in", "xt_full", "xgT_ready", "silu_ready", "act_ready",
                                                    "at_full", "actT_ready", "res_ready", "res_stored"))

        def full(eng, name):
            b, n = place[name]
            eng.wait_ge(bank_full[b], n)
            return ps[:, b]

        def taken(eng, name):
            b, n = place[name]
            eng.wait_ge(bank_out[b], n)

        def out_of(name):
            return bank_out[place[name][0]]

        block = ctx.enter_context(nc.Block())


        EW = ({"gate": 2, "up": 3, "down": 4}, {"gate": 5, "up": 0, "down": 1})
        TURNS = NE // 2
        w_src = {"gate": exp_w_gate[0].rearrange("e (p k) n -> e p (k n)", p=P),
                 "up": exp_w_up[0].rearrange("e (p k) n -> e p (k n)", p=P),
                 "down": exp_w_down[0].rearrange("e (k p) n -> e p k n", p=P)}
        B_XT, B_AT, B_GATE, B_UP, B_RES, B_RES2 = 0, 1, 2, 3, (6, 7), 4
        xt_bank = ps[:, B_XT].rearrange("p (k t) -> p k t", k=KD)
        at_bank = ps[:, B_AT, 0:256].rearrange("p (j n) -> p j n", j=2)
        HALF = F // 2

        def weights(eng, b, kind, e, signal):
            src = w_src[kind][e] if isinstance(e, int) else w_src[kind][bass.ds(e, 1)]
            dst = ring[:, EW[b][kind]]
            if kind == "down":
                dst = slot_h[EW[b][kind]]
                if not isinstance(e, int):
                    src = src.rearrange("e p k n -> p (e k) n")
            elif not isinstance(e, int):
                src = src.rearrange("e p n -> (e p) n")
            eng.dma_start(dst, src).then_inc(signal, 16)

        xg2, res2 = vb[0:CAP, 0:D], cb[:, 1536:2048]

        def turn_x(pe, rows):
            pe.sem_inc(passed, 1)
            v = rows.rearrange("t (p k) -> t k p", k=KD)
            for k in range(KD):
                t = nc.tensor.transpose(xt_bank[:, k], v[:, k], ident[0:CAP, 0:CAP])
            return t

        def hidden(b, kind, bank):
            w = slot_k[EW[b][kind]]
            for k in range(KD):
                for h in range(2):
                    t = nc.tensor.matmul(ps[CAP * h:CAP * (h + 1), bank, 0:HALF], xgT[b][:, k],
                                         w[:, k, HALF * h:HALF * (h + 1)], start=k == 0, stop=k == KD - 1)
            return t

        def turn_act(b):
            for j in range(2):
                t = nc.tensor.transpose(at_bank[:, j], act_[b][:, P * j:P * (j + 1)], ident[:])
            return t

        def down(b, bank):
            w = slot_h[EW[b]["down"]]
            for n, (h, j) in enumerate((h, j) for h in range(2) for j in range(2)):
                for c in range(2):
                    t = nc.tensor.matmul(ps[CAP * c:CAP * (c + 1), bank], actT[b][:, j, CAP * h:CAP * (h + 1)],
                                         w[:, 2 * h + j, W * c:W * (c + 1)], start=n == 0, stop=n == 3)
            return t

        def gain(b):
            return nc.vector.tensor_tensor(xgT[b], xt_bank, cols[:, GFX:GFX + KD].unsqueeze(2).to_broadcast((P, KD, CAP)), ALU.mult)

        def store_rows(eng, src, block, signal):
            for c in range(2):
                eng.dma_start(res_d[bass.ds(block * CAP, CAP), W * c:W * (c + 1)],
                              src[CAP * c:CAP * (c + 1)]).then_inc(signal, 16)

        def second_of(eng, e):
            at = [second[0:1, c, e:e + 1] if isinstance(e, int) else second[0:1, c, bass.ds(e, 1)] for c in range(2)]
            return eng.value_load(at[0], min_val=0, max_val=1), eng.value_load(at[1], min_val=0, max_val=NE)

        def each_over(eng, body):
            n = eng.value_load(ovi[0:1, NOV:NOV + 1], min_val=0, max_val=NOV)
            with eng.If(n > 0):
                body(0, True)
            with eng.Fori(1, NOV) as o_:
                with eng.If(n > o_):
                    body(o_, False)
            return n

        def experts_sync(sp):
            full(sp, ("br", 5, MW - 1))
            for kind in KINDS:
                weights(sp, 0, kind, 0, ew_in[0][kind])
            weights(sp, 1, "gate", 1, ew_in[1]["gate"])
            full(sp, ("o", NT - 1, 1))
            for kind in ("up", "down"):
                weights(sp, 1, kind, 1, ew_in[1][kind])
            for s in range(2):
                sp.wait_ge(h2_stored[s], 16 * 2)
            full(sp, ("rt", NT - 1, 1))
            sp.dma_start(hb[:, 0:D], norm_final_g.rearrange("(a d) -> a d", a=1).to_broadcast((P, D))).then_inc(gfin_in, 16)
            sp.wait_ge(ov_ready, 1)

            def second_through(b, e):
                flag, before = second_of(sp, e)
                sp.wait_ge(done2["down"], flag + before + 1)
                sp.sem_inc(passed, 1)

            with sp.Fori(1, TURNS) as i:
                for b in range(2):
                    second_through(b, i * 2 + (b - 2))
                    for kind in KINDS:
                        sp.wait_ge(done[b][kind], i)
                        weights(sp, b, kind, i * 2 + b, ew_in[b][kind])
            second_through(0, NE - 2)
            for kind in KINDS:
                sp.wait_ge(done[0][kind], TURNS)

            def over(o_, first):
                e = sp.value_load(ovi[0:1, bass.ds(o_, 1)] if not first else ovi[0:1, 0:1], min_val=0, max_val=NE - 1)
                for kind in KINDS:
                    if not first:
                        sp.wait_ge(ov_done[kind], o_)
                    weights(sp, 0, kind, e, ov_w)

            each_over(sp, over)
            for i in range(NT):
                sp.wait_ge(outrow_ready, i + 1)
                sp.dma_start(out[0, i * P:(i + 1) * P, :], x3[:, i]).then_inc(out_stored, 16)
            sp.wait_ge(out_stored, 16 * NT)

        def experts_tensor(pe):
            for b in range(8):
                pe.wait_ge(bank_out[b], max(n for bank, n in place.values() if bank == b))
            pe.sem_inc(done2["down"], 1)
            pe.sem_inc(xt2_full, 1)
            pe.wait_ge(xg_in[0], 16)
            turn_x(pe, xg[0]).then_inc(xt_full[0], 1)
            pe.wait_ge(ov_ready, 1)

            def turn(i, first):
                for b in range(2):
                    for kind, bank in (("gate", B_GATE), ("up", B_UP)):
                        pe.wait_ge(ew_in[b][kind], i * 16 + 16)
                        if kind == "gate":
                            pe.wait_ge(xgT_ready[b], i + 1)
                        hidden(b, kind, bank).then_inc(done[b][kind], 1)
                    pe.wait_ge(xg_in[1 - b], i * 16 + 16 + 16 * b)
                    turn_x(pe, xg[1 - b]).then_inc(xt_full[1 - b], 1)
                    pe.wait_ge(act_ready[b], i + 1)
                    turn_act(b).then_inc(at_full[b], 1)
                    pe.wait_ge(actT_ready[b], i + 1)
                    pe.wait_ge(ew_in[b]["down"], i * 16 + 16)
                    if not first:
                        pe.wait_ge(res_ready[b], i)
                    down(b, B_RES[b]).then_inc(done[b]["down"], 1)
                    flag, before = second_of(pe, i * 2 + b)
                    with pe.If(flag > 0):
                        pe.wait_ge(xg2_in, before * 16 + 16)
                        turn_x(pe, xg2).then_inc(xt2_full, 1)
                        pe.wait_ge(xgT2_ready, before + 1)
                        hidden(b, "gate", B_GATE).then_inc(done2["gate"], 1)
                        hidden(b, "up", B_UP).then_inc(done2["up"], 1)
                        pe.wait_ge(act2_ready, before + 1)
                        turn_act(b).then_inc(at2_full, 1)
                        pe.wait_ge(actT2_ready, before + 1)
                        down(b, B_RES2).then_inc(done2["down"], 1)
                        pe.wait_ge(res2_ready, before + 1)
                        pe.sem_inc(passed, 1)

            turn(0, True)
            with pe.Fori(1, TURNS) as i:
                turn(i, False)

            def over(o_, first):
                pe.wait_ge(ov_xg_in, o_ * 16 + 16)
                if first:
                    pe.wait_ge(xgT_ready[0], TURNS + 1)
                turn_x(pe, xg[0]).then_inc(ov_xt_full, 1)
                pe.wait_ge(ov_w, o_ * 48 + 48)
                pe.wait_ge(ov_xgT_ready, o_ + 1)
                if first:
                    pe.wait_ge(res_ready[0], TURNS)
                hidden(0, "gate", B_GATE).then_inc(ov_done["gate"], 1)
                hidden(0, "up", B_UP).then_inc(ov_done["up"], 1)
                pe.wait_ge(ov_act_ready, o_ + 1)
                turn_act(0).then_inc(ov_at_full, 1)
                pe.wait_ge(ov_actT_ready, o_ + 1)
                if not first:
                    pe.wait_ge(ov_res_ready, o_)
                down(0, B_RES[0]).then_inc(ov_done["down"], 1)

            each_over(pe, over)

        def experts_vector(v):
            v.wait_ge(xt_full[0], 1)
            gain(0).then_inc(xgT_ready[0], 1)

            def turn(i, first):
                for b in range(2):
                    v.wait_ge(silu_ready[b], i + 1)
                    v.wait_ge(done[b]["up"], i + 1)
                    if not first:
                        v.wait_ge(at_full[b], i)
                    nc.vector.tensor_tensor(act_[b], silu[b], ps[:, B_UP, 0:HALF], ALU.mult).then_inc(act_ready[b], 1)
                    v.wait_ge(xt_full[1 - b], i + 1 + b)
                    if b == 1 or not first:
                        v.wait_ge(done[1 - b]["up"], i + b)
                    gain(1 - b).then_inc(xgT_ready[1 - b], 1)
                    v.wait_ge(at_full[b], i + 1)
                    if not first:
                        v.wait_ge(done[b]["down"], i)
                    nc.vector.tensor_copy(actT[b], at_bank).then_inc(actT_ready[b], 1)
                    flag, before = second_of(v, i * 2 + b)
                    with v.If(flag > 0):
                        v.wait_ge(xt2_full, before + 2)
                        gain(b).then_inc(xgT2_ready, 1)
                        v.wait_ge(silu2_ready, before + 1)
                        v.wait_ge(done2["up"], before + 1)
                        nc.vector.tensor_tensor(act_[b], silu[b], ps[:, B_UP, 0:HALF], ALU.mult).then_inc(act2_ready, 1)
                        v.wait_ge(at2_full, before + 1)
                        nc.vector.tensor_copy(actT[b], at_bank).then_inc(actT2_ready, 1)

            turn(0, True)
            with v.Fori(1, TURNS) as i:
                turn(i, False)

            def over(o_, first):
                v.wait_ge(ov_xt_full, o_ + 1)
                if first:
                    v.wait_ge(done[0]["up"], TURNS)
                gain(0).then_inc(ov_xgT_ready, 1)
                v.wait_ge(ov_silu_ready, o_ + 1)
                v.wait_ge(ov_done["up"], o_ + 1)
                nc.vector.tensor_tensor(act_[0], silu[0], ps[:, B_UP, 0:HALF], ALU.mult).then_inc(ov_act_ready, 1)
                v.wait_ge(ov_at_full, o_ + 1)
                if first:
                    v.wait_ge(done[0]["down"], TURNS)
                nc.vector.tensor_copy(actT[0], at_bank).then_inc(ov_actT_ready, 1)

            each_over(v, over)
            v.wait_ge(gfin_in, 16)

            def final_norm(i):
                v.wait_ge(std3_ready, i + 1)
                nc.vector.reciprocal(stat[:, 24 + i:25 + i], stat[:, 20 + i:21 + i]).then_inc(fin_step, 1)
                v.wait_ge(fin_step, i + 1)
                nc.vector.scalar_tensor_tensor(x3[:, i], x3[:, i], stat[:, 24 + i:25 + i], hb[:, 0:D],
                                               ALU.mult, ALU.mult).then_inc(outrow_ready, 1)

            for i in range(NT):
                v.wait_ge(picked[i], 32)
                for c in range(2):
                    nc.vector.scalar_tensor_tensor(x3[:, i], picked_rows(i, c), wts[:, NT * c + i:NT * c + i + 1], x3[:, i],
                                                   ALU.mult, ALU.add).then_inc(sums_ready, 1)
                    v.wait_ge(sums_ready, 2 * i + c + 1)
                if i >= 1:
                    final_norm(i - 1)
            final_norm(NT - 1)

        def experts_scalar(act):
            def results(dst, bank, block, full_sem, full_n, ready, ready_n, stored, stored_n):
                act.wait_ge(full_sem, full_n)
                if stored_n is not None:
                    act.wait_ge(stored, stored_n)
                nc.scalar.copy(dst, ps[:, bank]).then_inc(ready, 1)
                act.wait_ge(ready, ready_n)
                store_rows(act, dst, block, stored)

            def turn(i, first):
                for b in range(2):
                    act.wait_ge(done[b]["gate"], i + 1)
                    if not first:
                        act.wait_ge(act_ready[b], i)
                    nc.scalar.activation(silu[b], ps[:, B_GATE, 0:HALF], ACT.Silu).then_inc(silu_ready[b], 1)
                    results(res[b], B_RES[b], i * 2 + b, done[b]["down"], i + 1, res_ready[b], i + 1, res_stored[b],
                            None if first else i * 32)
                    flag, before = second_of(act, i * 2 + b)
                    with act.If(flag > 0):
                        act.wait_ge(done2["gate"], before + 1)
                        nc.scalar.activation(silu[b], ps[:, B_GATE, 0:HALF], ACT.Silu).then_inc(silu2_ready, 1)
                        results(res2, B_RES2, i * 2 + (b + NE), done2["down"], before + 2, res2_ready, before + 1,
                                res2_stored, before * 32 + 1)

            act.wait_ge(ov_ready, 1)
            act.sem_inc(res2_stored, 1)
            turn(0, True)
            with act.Fori(1, TURNS) as i:
                turn(i, False)

            def over(o_, first):
                act.wait_ge(ov_done["gate"], o_ + 1)
                if first:
                    act.wait_ge(act_ready[0], TURNS)
                else:
                    act.wait_ge(ov_act_ready, o_)
                nc.scalar.activation(silu[0], ps[:, B_GATE, 0:HALF], ACT.Silu).then_inc(ov_silu_ready, 1)
                if first:
                    act.wait_ge(res_stored[0], TURNS * 32)
                results(res[0], B_RES[0], o_ + 2 * NE, ov_done["down"], o_ + 1, ov_res_ready, o_ + 1, ov_res_stored, None if first else o_ * 32)

            each_over(act, over)
            flag, before = second_of(act, NE - 1)
            act.wait_ge(res2_stored, (flag + before) * 32 + 1)
            act.sem_inc(results_stored, 1)
            for i in range(NT):
                act.wait_ge(sums_ready, 2 * i + 2)
                nc.scalar.activation(ring[:, 0, 0:D], x3[:, i], ACT.Square, accum_out=stat[:, 16 + i:17 + i]).then_inc(ssq3_ready, 1)
                act.wait_ge(ssq3_ready, i + 1)
                nc.scalar.activation(stat[:, 20 + i:21 + i], stat[:, 16 + i:17 + i], ACT.Sqrt, scale=1.0 / D,
                                     bias=eps).then_inc(std3_ready, 1)

        def picked_rows(i, c):
            at = D * (2 * (i % 2) + c)
            return (mb if i < 2 else ring[:, EW[1]["gate"]])[:, at:at + D]

        def gather_rows(dst, table_, idx, signal):
            nc.gpsimd.indirect_dma_start(dst, None, table_, bass.IndirectOffsetOnAxis(ap=idx, axis=0)).then_inc(signal, 16)

        def experts_gpsimd(gp):
            gp.wait_ge(idx_ready, 1)
            for s in range(2):
                gp.wait_ge(h2_stored[s], 16 * 2)

            def fetch(e, b, count, signal, copied, side):
                src = idx_u[:, e:e + 1] if isinstance(e, int) else idx_u[:, bass.ds(e, 1)]
                nc.gpsimd.tensor_copy(idx_now[:, side:side + 1], src).then_inc(copied, 1)
                gp.wait_ge(copied, count)
                gp.sem_inc(passed, 1)
                gather_rows(xg[b] if b is not None else xg2, h2_d, idx_now[:, side:side + 1], signal)

            def fetch_second(e):
                flag, before = second_of(gp, e)
                with gp.If(flag > 0):
                    gp.wait_ge(xt2_full, before + 1)
                    gp.sem_inc(passed, 1)
                    fetch(e + NE, None, before + 1, xg2_in, idx2_copied, 3)

            gp.wait_ge(ov_ready, 1)
            for b in range(2):
                fetch(b, b, b + 1, xg_in[b], idx_copied, b)
            with gp.Fori(1, TURNS) as i:
                for b in range(2):
                    fetch_second(i * 2 + (b - 2))
                    gp.wait_ge(xt_full[b], i)
                    fetch(i * 2 + b, b, i * 2 + b + 1, xg_in[b], idx_copied, b)
            fetch_second(NE - 2)
            gp.wait_ge(xt_full[0], TURNS)
            fetch(NE, 0, NE + 1, xg_in[0], idx_copied, 0)
            fetch_second(NE - 1)
            gp.wait_ge(xt_full[0], TURNS + 1)

            def over(o_, first):
                if not first:
                    gp.wait_ge(ov_xt_full, o_)
                fetch(o_ + 2 * NE, 0, o_ + 1, ov_xg_in, ov_idx_copied, 2)

            n = each_over(gp, over)
            gp.wait_ge(results_stored, 1)
            for b in range(2):
                gp.wait_ge(res_stored[b], TURNS * 32)
            with gp.If(n > 0):
                gp.wait_ge(ov_res_stored, n * 32)
                gp.sem_inc(passed, 1)
            for i in range(NT):
                for c in range(2):
                    gather_rows(picked_rows(i, c), res_d, row_u[:, NT * c + i:NT * c + i + 1], picked[i])

        @block.sync
        def _(sp):
            for i, a in enumerate((ssm_a_re, ssm_a_im)):
                sp.dma_start(par_nat[:, i].rearrange("q (two p) -> q two p", two=2),
                             a[0].rearrange("(two q) p -> q two p", two=2)).then_inc(params_in, 16)
            sp.dma_start(ldt_nat, ssm_log_dt[0].rearrange("(two q) -> q two", two=2)).then_inc(params_in, 16)
            for r, c in enumerate((ssm_c_re, ssm_c_im)):
                for t in range(2):
                    sp.dma_start(c_nat[r][:, t].rearrange("p (two s) -> p two s", two=2),
                                 c[0].rearrange("(two t q) c s -> t (q c) two s", two=2, t=2)[t]).then_inc(params_in, 16)
            sp.dma_start(sgw_nat, sgu_w[0].rearrange("h t s -> t h s")).then_inc(params_in, 16)
            for i in range(NT):
                sp.dma_start(x3[:, i], x[0, i * P:(i + 1) * P, :]).then_inc(x_in[i], 16)

            def load_win(n, last=None):
                if last:
                    full(sp, last)
                src = (w_in[0][:, WIN_COLS[n]:WIN_COLS[n] + W] if n < 10 else w_out[0][:, (n - 10) * W:(n - 9) * W])
                sp.dma_start(slot_k[n % 2], src.rearrange("(k p) n -> p k n", p=P)).then_inc(win_in[n % 2], 16)

            def load_wb(n, last=None):
                half, k = GATE_STEPS[n]
                if last:
                    full(sp, last)
                sp.dma_start(wb_slot[n % 2], w_branch[0, k][:, half * W:(half + 1) * W].rearrange(
                    "(k p) n -> p k n", p=P)).then_inc(wb_in[n % 2], 16)

            sp.dma_start(cols[:, GMX:GMX + KD], norm_mix_g[0].rearrange("(k p) -> p k", p=P)).then_inc(b_in, 16)
            for r, b in enumerate((ssm_b_re, ssm_b_im)):
                for two in range(2):
                    sp.dma_start(b_raw[r][two * S:(two + 1) * S],
                                 b[0, two * Q:(two + 1) * Q].rearrange("q s c -> s q c")).then_inc(b_in, 16)
            load_win(0)
            load_win(1)
            sp.dma_start(cols[:, BG:BG + 24], b_gate[0].rearrange("(k p) -> p k", p=P)).then_inc(consts_in, 16)
            for at, v, k in ((GB, glu_b, 4), (PSC, pool_scale, 4), (DSK, ssm_d, 4), (GFF, norm_ffn_g, KD)):
                sp.dma_start(cols[:, at:at + k], v[0].rearrange("(k p) -> p k", p=P)).then_inc(consts_in, 16)
            sp.dma_start(cols[:, GFX:GFX + KD], norm_ffn_g[0].rearrange("(p k) -> p k", p=P)).then_inc(consts_in, 16)
            sp.dma_start(poolw, pool_w[0].rearrange("g c d -> c g d")).then_inc(consts_in, 16)
            sp.dma_start(bs_row[:], sgu_b[0:1]).then_inc(consts_in, 16)
            sp.dma_start(rbias[:, 0:4], router_group_b[0:1]).then_inc(consts_in, 16)
            sp.dma_start(rbias[:, 4:36], router_expert_b[0:1]).then_inc(consts_in, 16)
            sp.dma_start(lng, sgu_ln_g[0:1].to_broadcast((P, W))).then_inc(consts_in, 16)
            sp.dma_start(lnb, sgu_ln_b[0:1].to_broadcast((P, W))).then_inc(consts_in, 16)

            taken(sp, ("c", MW - 1))
            sp.dma_start(xc_d.rearrange("(m p) t -> p m t", p=P), C).then_inc(xc_stored, 16)
            load_win(2, ("c", MW - 1))
            sp.wait_ge(xc_stored, 16)
            for j in range(J):
                sp.dma_start(u8v[CH * j:CH * (j + 1)],
                             xc_d.rearrange("(g c) (j n) -> j c g n", c=CH, j=J)[j]).then_inc(u8_in, 16)
            load_win(3, ("a", MW - 1))
            taken(sp, ("k", 7))
            sp.wait_ge(toep_zero, 1)
            n_rows = (NB - NE) * CAP
            for r in range(0, n_rows, 4 * P):
                n = min(4 * P, n_rows - r)
                sp.dma_start(res_d[NE * CAP + r:NE * CAP + r + n, :].rearrange("(p r) d -> p (r d)", r=4),
                             xb[0:n // 4, :]).then_inc(over_zero, 16)
            sp.wait_ge(over_zero, 16 * ((n_rows + 4 * P - 1) // (4 * P)))
            for i in range(J):
                sp.dma_start(toep[CH * i:CH * (i + 1), :, CH * i:P], ker[:, :, 0:P - CH * i]).then_inc(ker_in, 16)
            sp.wait_ge(ker_in, 16 * J)
            sp.dma_start(gluw, glu_w[0].rearrange("(k p) n -> p k n", p=P)).then_inc(glu_in, 16)
            load_wb(0, ("bu", 1, 1))
            load_wb(1, ("bu", 1, 1))
            load_win(4, ("u", MW - 1))
            taken(sp, ("y", 3))
            for j in range(J):
                sp.dma_start(y_d.rearrange("(g c) (j n) -> j c g n", c=CH, j=J)[j],
                             y8v[CH * j:CH * (j + 1)]).then_inc(y_stored, 16)
            sp.wait_ge(y_stored, 16 * J)
            sp.dma_start(yT, y_d.rearrange("(m p) t -> p m t", p=P)).then_inc(yT_in, 16)
            load_win(5, ("v", NT - 1))
            full(sp, ("sg", 3))
            sp.dma_start(rw[:, :, 0:4], router_group_w[0].rearrange("(k p) n -> p k n", p=P)).then_inc(router_in, 16)
            sp.dma_start(rw[:, :, 4:36], router_expert_w[0].rearrange("(k p) n -> p k n", p=P)).then_inc(router_in, 16)
            for n in range(2, 8):
                sp.wait_ge(w_lo_ready, 2 * (n - 1))
                load_win(4 + n)
                if n < 6:
                    load_wb(n)
            full(sp, ("gt", 5, MW - 1))
            sp.dma_start(x3, x[0].rearrange("(i p) d -> p i d", p=P)).then_inc(x_again, 16)
            experts_sync(sp)

        @block.tensor
        def _(pe):
            def start(name):
                b, n = place[name]
                if n > 1:
                    pe.wait_ge(bank_out[b], n - 1)
                return ps[:, b]

            def end(name, ins):
                ins.then_inc(bank_full[place[name][0]], 1)

            def turn(name, ins_, ready=None):
                bank, at = start(name), 0
                for a in ins_:
                    n, w = a.shape[0], a.shape[1]
                    t = nc.tensor.transpose(bank[0:w, at:at + n], a, ident[0:n, 0:n])
                    at += n
                end(name, t)

            def product(name, pairs, cols_=512):
                bank = start(name)
                for i, (lhs, rhs) in enumerate(pairs):
                    t = nc.tensor.matmul(bank[0:lhs.shape[1], 0:cols_], lhs, rhs, start=i == 0, stop=i == len(pairs) - 1)
                end(name, t)

            pe.wait_ge(ident_ready, 1)
            pe.wait_ge(params_in, 16 * 8)
            pe.wait_ge(ldt_spread, 1)
            turn("par", [par_nat[:, i] for i in range(3)])
            turn("ct", [c_nat[r][:, t] for r in range(2) for t in range(2)])
            pe.wait_ge(sgw_masked, 1)
            turn("wst", [sgw_nat[:, h] for h in range(4)])
            for i in range(NT):
                pe.wait_ge(xn_ready, i + 1)
                for h in range(2):
                    turn(("x", i, h), [x3[:, i, (4 * h + k) * P:(4 * h + k + 1) * P] for k in range(4)])
            taken(pe, ("x", NT - 1, 1))

            def channels(tag, n):
                pe.wait_ge(win_in[n % 2], 16 * (n // 2 + 1))
                for m in range(MW):
                    product((*tag, m), [(slot_k[n % 2][:, k, m * P:(m + 1) * P], hT[:, k]) for k in range(KD)])

            channels(("c",), 0)
            channels(("a",), 1)
            pe.wait_ge(btpre_ready, 1)
            for r in range(2):
                for i in range(4):
                    turn(("bt", r, i), [bt_pre[r][:, q].rearrange("p j c -> p (j c)") for q in range(4 * i, 4 * i + 4)])
            pe.wait_ge(cp_ready, 1)
            for i in range(8):
                bank = start(("k", i))
                for g in range(4 * i, 4 * i + 4):
                    rows, q = slice(S * (g // Q), S * (g // Q + 1)), g % Q
                    o_ = bank[0:CH, P * (g % 4):P * (g % 4 + 1)]
                    nc.tensor.matmul(o_, b_bar[0][rows, q], cp_re[rows, q, 0:J].rearrange("p j c -> p (j c)"), start=True, stop=False)
                    t = nc.tensor.matmul(o_, b_bar[1][rows, q], cp_im[rows, q, 0:J].rearrange("p j c -> p (j c)"), start=False, stop=True)
                end(("k", i), t)
            pe.wait_ge(u8_in, 16 * J)
            taken(pe, ("bt", 1, 3))
            for h in range(2):
                for r in range(2):
                    bank = start(("bu", h, r))
                    for q in range(8 * h, 8 * h + 8):
                        for two in range(2):
                            t = nc.tensor.matmul(bank[S * two:S * (two + 1), NC * (q % 8):NC * (q % 8 + 1)],
                                                 btT[r][:, q, S * two:S * (two + 1)], u8v[:, two * Q + q], start=True, stop=True)
                    end(("bu", h, r), t)
            channels(("u",), 2)
            pe.wait_ge(ker_in, 16 * J)
            pe.wait_ge(st_ready, 1)
            for i in range(4):
                bank = start(("y", i))
                for g in range(8 * i, 8 * i + 8):
                    rows, q = slice(S * (g // Q), S * (g // Q + 1)), g % Q
                    o_ = bank[:, NC * (g % 8):NC * (g % 8 + 1)]
                    nc.tensor.matmul(o_, toep[:, g], u8v[:, g], start=True, stop=False)
                    nc.tensor.matmul(o_, cp_re[rows, q, 1:J + 1].rearrange("p j c -> p (j c)"), st_re[rows, q], start=False, stop=False)
                    t = nc.tensor.matmul(o_, cp_im[rows, q, 1:J + 1].rearrange("p j c -> p (j c)"), st_im[rows, q], start=False, stop=True)
                end(("y", i), t)
            pe.wait_ge(win_in[1], 16 * 2)
            for i in range(NT):
                product(("v", i), [(hT[:, k, i * P:(i + 1) * P], slot_k[1][:, k]) for k in range(KD)])
            pe.wait_ge(glu_in, 16)
            pe.wait_ge(yg_ready, MW)
            for m in range(MW):
                product(("gl", m), [(gluw[:, k, m * P:(m + 1) * P], C[:, k]) for k in range(MW)])
            pe.wait_ge(consts_in, 16 * 12)
            for m in range(MW):
                pe.wait_ge(diff_ready, m + 1)
                product(("py", m), [(poolw[:, m], A[:, m])])
            pe.wait_ge(vn_ready, NT)
            pe.wait_ge(consts_made, 1)
            for h in range(4):
                bank = start(("sg", h))
                for n in range(NT):
                    nc.tensor.matmul(bank[:, n * P:(n + 1) * P], ones_row[:], bs_row[0:1, h], start=True, stop=False)
                    t = nc.tensor.matmul(bank[:, n * P:(n + 1) * P], V[:, n, h * P:(h + 1) * P], wst[:, h], start=False, stop=True)
                end(("sg", h), t)
            def split(w_hi, w_lo, x_hi, x_lo, n, cs):
                return [(w[:, k, cs], x_[:, k]) for k in range(n) for w, x_ in ((w_hi, x_hi), (w_hi, x_lo), (w_lo, x_hi))]

            pe.wait_ge(h_lo_ready, 1)
            for n, (half, k_) in enumerate(GATE_STEPS):
                for m in range(MW):
                    s, cs = m // 2, slice(P * (m % 2), P * (m % 2 + 1))
                    if m % 2 == 0:
                        pe.wait_ge(w_lo_ready, 2 * n + s + 1)
                    product(("gt", n, m), split(wg_hi[s], wg_lo[s], h_hi, h_lo, KD, cs))
                    if m == 0 and half == 0:
                        pe.wait_ge(y_lo_ready, k_ + 1)
                    product(("br", n, m), split(wb_hi[s], wb_lo[s], y_hi, y_lo[k_], MW, cs))
            taken(pe, ("br", 5, MW - 1))
            for s in range(2):
                pe.wait_ge(win_in[s], 16 * 6)

            def route(i):
                pe.wait_ge(h2_ready, i + 1)
                for h in range(2):
                    turn(("rt", i, h), [h2n[i % 2][:, (4 * h + k) * P:(4 * h + k + 1) * P] for k in range(4)])
                taken(pe, ("rt", i, 1))
                product(("lg", i), [(h2T[:, k], rw[:, k]) for k in range(KD)] + [(ones_row[:], rbias[:])], 36)

            pe.wait_ge(router_in, 32)
            for i in range(NT):
                for h in range(2):
                    product(("o", i, h), [(M[:, k, i * P:(i + 1) * P], slot_k[h][:, k]) for k in range(KD)])
                if i >= 1:
                    route(i - 1)
            route(NT - 1)
            pe.wait_ge(onehot_ready, 1)
            pe.wait_ge(masks_ready, 1)
            bank = start("pos")
            tri, ones = lng[:, 0:P], lnb[:, 0:P]
            for i in range(NT):
                for i2 in range(i + 1):
                    nc.tensor.matmul(bank[:, NE * i:NE * (i + 1)], tri if i2 == i else ones, oh[:, i2], start=i2 == 0, stop=i2 == i)
            for i in range(NT):
                t = nc.tensor.matmul(bank[:, NE * NT:NE * (NT + 1)], ones, oh[:, i], start=i == 0, stop=i == NT - 1)
            end("pos", t)
            pe.wait_ge(tok_in, 16)
            turn("tok", [tok_rows])
            experts_tensor(pe)

        @block.scalar
        def _(act):
            def copy_out(name, dst, rows=P, cols_=512):
                nc.scalar.copy(dst, full(act, name)[0:rows, 0:cols_]).then_inc(out_of(name), 1)

            copy_out("par", prm[:, 0:3].rearrange("p n q -> p (n q)"), cols_=48)
            copy_out("ct", ub[:, 1024:1536])
            taken(act, "par")
            nc.scalar.activation(c_("dt"), c_("ldt"), ACT.Exp).then_inc(dt_ready, 1)
            for i in range(NT):
                act.wait_ge(x_in[i], 16)
                nc.scalar.activation(mb[:, 1024 * i:1024 * (i + 1)], x3[:, i], ACT.Square,
                                     accum_out=stat[:, i:i + 1]).then_inc(ssq_ready, 1)
            act.wait_ge(ssq_ready, NT)
            act.wait_ge(consts_made, 1)
            nc.scalar.activation(stat[:, 4:8], stat[:, 0:4], ACT.Sqrt, scale=1.0 / D, bias=eps).then_inc(std_ready, 1)
            act.wait_ge(angle_ready, 1)
            nc.scalar.activation(c_("e1"), c_("r"), ACT.Exp).then_inc(act_prm, 1)
            nc.scalar.activation(c_("rho"), c_("r"), ACT.Exp, scale=float(J)).then_inc(act_prm, 1)
            nc.scalar.activation(c_("tanh"), c_("r"), ACT.Tanh, scale=0.5).then_inc(act_prm, 1)
            nc.scalar.activation(c_("s"), c_("nhalf"), ACT.Sin).then_inc(act_prm, 1)
            nc.scalar.activation(c_("c"), c_("ab"), ACT.Sin).then_inc(act_prm, 1)
            copy_out("wst", wst.rearrange("p h t -> p (h t)"))
            for m in range(MW):
                name = ("c", m)
                nc.scalar.copy(C[:, m].rearrange("p (j c) -> p c j", j=J),
                               full(act, name).rearrange("p (c j) -> p c j", j=J)).then_inc(out_of(name), 1)
            for m in range(MW):
                copy_out(("a", m), A[:, m])
            for r in range(2):
                for i in range(4):
                    copy_out(("bt", r, i), btT[r][:, 4 * i:4 * i + 4].rearrange("p q n -> p (q n)"))
            for i in range(8):
                copy_out(("k", i), ker[:, 4 * i:4 * i + 4].rearrange("p g n -> p (g n)"), rows=CH)
            for m in range(MW):
                name = ("u", m)
                nc.scalar.activation(U[:, m], full(act, name), ACT.Gelu_apprx_tanh).then_inc(out_of(name), 1)
            act.wait_ge(st_ready, 1)
            for i in range(4):
                copy_out(("y", i), y8v[:, 8 * i:8 * i + 8].rearrange("p g c -> p (g c)"))
            for i in range(NT):
                name = ("v", i)
                nc.scalar.activation(V[:, i], full(act, name), ACT.Gelu_apprx_tanh).then_inc(out_of(name), 1)
            for m in range(MW):
                act.wait_ge(ych_ready, m + 1)
                nc.scalar.activation(C[:, m].rearrange("p (c j) -> p c j", j=J),
                                     yT[:, m].rearrange("p (j c) -> p c j", j=J), ACT.Gelu_apprx_tanh).then_inc(yg_ready, 1)
            act.wait_ge(var_ready, 1)
            nc.scalar.activation(stat[:, 40:44], stat[:, 32:36], ACT.Sqrt, bias=eps).then_inc(vstd_ready, 1)
            full(act, ("y", 3))
            nc.scalar.copy(h_hi[:], hT).then_inc(h_hi_ready, 1)
            act.wait_ge(yg_ready, MW)
            act.wait_ge(consts_in, 16 * 12)
            for m in range(MW):
                name = ("gl", m)
                nc.scalar.activation(yT[:, m], full(act, name), ACT.Sigmoid, bias=cols[:, GB + m:GB + m + 1]).then_inc(out_of(name), 1)

            def upper(n, s):
                act.wait_ge(win_in[n % 2], 16 * ((4 + n) // 2 + 1))
                act.wait_ge(wb_in[n % 2], 16 * (n // 2 + 1))
                if n >= 1:
                    full(act, ("br", n - 1, 2 * s + 1))
                nc.scalar.copy(wg_hi[s][:], slot_k[n % 2][:, :, SW * s:SW * (s + 1)]).then_inc(w_hi_ready, 1)
                nc.scalar.copy(wb_hi[s][:], wb_slot[n % 2][:, :, SW * s:SW * (s + 1)]).then_inc(w_hi_ready, 1)

            act.wait_ge(yc_ready, MW)
            upper(0, 0)
            upper(0, 1)
            for m in range(MW):
                name = ("py", m)
                nc.scalar.activation(A[:, m], full(act, name), ACT.Copy, scale=cols[:, PSC + m:PSC + m + 1]).then_inc(out_of(name), 1)
            taken(act, ("py", MW - 1))
            full(act, ("sg", 3))
            for n, (half, k_) in enumerate(GATE_STEPS):
                if half == 0:
                    if k_ == 1:
                        taken(act, ("sg", 3))
                    if k_ >= 1:
                        full(act, ("br", n - 1, MW - 1))
                    nc.scalar.copy(y_hi[:], (A, U, C)[k_]).then_inc(y_hi_ready, 1)
                for m in range(MW):
                    i = n * MW + m
                    col = BG + k_ * KD + half * MW + m
                    if i >= 2:
                        act.wait_ge(merge_done, i - 1)
                    name = ("gt", n, m)
                    nc.scalar.activation(sig[i % 2], full(act, name), ACT.Sigmoid, bias=cols[:, col:col + 1]).then_inc(out_of(name), 1)
                    if m % 2 == 1 and n < 5:
                        upper(n + 1, m // 2)
            for i in range(NT):
                taken(act, ("o", i, 1))
                nc.scalar.activation(cb[:, 0:1024], x3[:, i], ACT.Square, accum_out=stat[:, 8 + i:9 + i]).then_inc(ssq2_ready, 1)
                act.wait_ge(ssq2_ready, i + 1)
                nc.scalar.activation(stat[:, 12 + i:13 + i], stat[:, 8 + i:9 + i], ACT.Sqrt, scale=1.0 / D,
                                     bias=eps).then_inc(std2_ready, 1)
            act.wait_ge(exp_in, 1)
            nc.scalar.activation(R["ex4"], R["dg"], ACT.Exp).then_inc(exp_out, 1)
            act.wait_ge(exp2_in, 1)
            nc.scalar.activation(R["ex"], R["dm"], ACT.Exp).then_inc(exp2_out, 1)
            experts_scalar(act)

        @block.vector
        def _(v):
            vv = nc.vector
            step = Steps(v, dve_step)
            then, mark = step.then, step.mark

            def mul(o_, a, b):
                return vv.tensor_tensor(o_, a, b, ALU.mult)

            def add(o_, a, b):
                return vv.tensor_tensor(o_, a, b, ALU.add)

            def sub(o_, a, b):
                return vv.tensor_tensor(o_, a, b, ALU.subtract)

            def axpy(o_, a, k, b, op=ALU.add):
                return vv.scalar_tensor_tensor(o_, a, k, b, ALU.mult, op)

            def cmul(o_re, o_im, a, b, t, conj=False, neg_im=False):
                mark(mul(t, a[1], b[1]))
                then(mul(o_re, a[0], b[0]))
                then((add if conj else sub)(o_re, o_re, t))
                mark(mul(t, a[0], b[1]))
                then(mul(o_im, a[1], b[0]))
                if neg_im:
                    then(axpy(o_im, o_im, -1.0, t, ALU.subtract))
                else:
                    then((sub if conj else add)(o_im, o_im, t))

            C1 = 6.28125
            C2 = 0.0019350051879882812
            C3 = 2 * math.pi - C1 - C2
            taken(v, "par")
            v.wait_ge(dt_ready, 1)
            mark(mul(c_("r"), c_("are"), c_("dt")))
            then(mul(c_("th"), c_("aim"), c_("dt")))
            then(vv.tensor_scalar(c_("n"), c_("th"), 1.0 / (2 * math.pi), MAGIC, ALU.mult, ALU.add))
            then(vv.tensor_scalar(c_("n2"), c_("n"), -MAGIC, None, ALU.add))
            then(axpy(c_("t1"), c_("n2"), -C1, c_("th")))
            then(axpy(c_("t2"), c_("n2"), -C2, c_("t1")))
            then(axpy(c_("thr"), c_("n2"), -C3, c_("t2")))
            then(vv.tensor_scalar(c_("nhalf"), c_("thr"), 0.5, None, ALU.mult))
            then(axpy(c_("t3"), c_("nhalf"), -1.0, c_("nhalf"), ALU.max))
            vv.tensor_scalar(c_("ab"), c_("t3"), -1.0, math.pi / 2, ALU.mult, ALU.add).then_inc(angle_ready, 1)
            mark(mul(c_("t1"), c_("are"), c_("are")))
            then(mul(c_("t2"), c_("aim"), c_("aim")))
            then(add(c_("m2"), c_("t1"), c_("t2")))
            then(vv.reciprocal(c_("inv"), c_("m2")))

            v.wait_ge(std_ready, 1)
            then(vv.reciprocal(stat[:, 28:32], stat[:, 4:8]))
            v.wait_ge(b_in, 16 * 5)

            def spread_out(i):
                for h in range(2):
                    name = ("x", i, h)
                    bank = full(v, name).rearrange("p (k t) -> p k t", k=4)
                    vv.tensor_tensor(hT[:, 4 * h:4 * h + 4, i * P:(i + 1) * P], bank,
                                     cols[:, GMX + 4 * h:GMX + 4 * h + 4].unsqueeze(2).to_broadcast((P, 4, P)),
                                     ALU.mult).then_inc(out_of(name), 1)

            for i in range(NT):
                vv.tensor_scalar(x3[:, i], x3[:, i], stat[:, 28 + i:29 + i], None, ALU.mult).then_inc(xn_ready, 1)
                if i >= 1:
                    spread_out(i - 1)
            spread_out(NT - 1)

            v.wait_ge(act_prm, 5)
            mark(vv.tensor_scalar(c_("one_m"), c_("tanh"), -1.0, 1.0, ALU.mult, ALU.add))
            mark(vv.scalar_tensor_tensor(c_("cosm1"), c_("s"), -2.0, c_("s"), ALU.mult, ALU.mult))
            then(vv.scalar_tensor_tensor(c_("sin"), c_("s"), 2.0, c_("c"), ALU.mult, ALU.mult))
            mark(vv.reciprocal(c_("t1"), c_("one_m")))
            then(vv.tensor_scalar(c_("cos"), c_("cosm1"), 1.0, None, ALU.add))
            mark(vv.memset(pw_re[:, 0], 1.0))
            mark(vv.memset(pw_im[:, 0], 0.0))
            mark(mul(pw_re[:, 1], c_("e1"), c_("cos")))
            mark(mul(pw_im[:, 1], c_("e1"), c_("sin")))
            then(vv.scalar_tensor_tensor(c_("em1"), c_("tanh"), 2.0, c_("t1"), ALU.mult, ALU.mult))
            then(mul(c_("t2"), c_("em1"), c_("cos")))
            then(add(c_("nr"), c_("t2"), c_("cosm1")))
            cmul(c_("t1"), c_("t2"), (c_("nr"), pw_im[:, 1]), (c_("are"), c_("aim")), c_("t3"), conj=True)
            mark(mul(c_("wr"), c_("t1"), c_("inv")))
            then(mul(c_("wi"), c_("t2"), c_("inv")))
            for lo, hi, base in ((2, 3, 1), (3, 5, 2), (5, 9, 4)):
                n = hi - lo
                k = (P, n, Q)
                cmul(pw_re[:, lo:hi], pw_im[:, lo:hi], (pw_re[:, lo - base:hi - base], pw_im[:, lo - base:hi - base]),
                     (pw_re[:, base:base + 1].to_broadcast(k), pw_im[:, base:base + 1].to_broadcast(k)), pwrev[:, 0, 0:n])
            for m in range(J):
                mark(vv.tensor_copy(pwrev[:, 0, m], pw_re[:, J - 1 - m]))
                mark(vv.tensor_copy(pwrev[:, 1, m], pw_im[:, J - 1 - m]))
            sc = (P, Q, CH)
            tsmall = ctmp[:, 0:Q * CH].rearrange("p (q c) -> p q c", q=Q)
            cmul(b_bar[0], b_bar[1], b_raw, (c_("wr").unsqueeze(2).to_broadcast(sc), c_("wi").unsqueeze(2).to_broadcast(sc)), tsmall)
            sh = (P, Q, J, CH)
            tb = ctmp[:, 0:Q * J * CH].rearrange("p (q j c) -> p q j c", q=Q, j=J)
            cmul(bt_pre[0], bt_pre[1], [b.unsqueeze(2).to_broadcast(sh) for b in b_bar],
                 [pwrev[:, r].rearrange("p j q -> p q j").unsqueeze(3).to_broadcast(sh) for r in range(2)], tb)
            vv.tensor_copy(stat[:, 61:62], stat[:, 28:29]).then_inc(btpre_ready, 1)
            taken(v, "ct")
            sh = (P, Q, J + 1, CH)
            tc_ = ctmp.rearrange("p (q j c) -> p q j c", q=Q, j=J + 1)
            cmul(cp_re, cp_im, [c.unsqueeze(2).to_broadcast(sh) for c in c_T],
                 [w.rearrange("p j q -> p q j").unsqueeze(3).to_broadcast(sh) for w in (pw_re[:], pw_im[:])], tc_, neg_im=True)
            vv.tensor_copy(stat[:, 61:62], stat[:, 28:29]).then_inc(cp_ready, 1)
            ph = [(c_("cos"), c_("sin")), (c_("cr1"), c_("ci1")), (c_("cr2"), c_("ci2"))]
            src = 0
            for n in range(3):
                dst = 1 if src != 1 else 2
                cmul(*ph[dst], ph[src], ph[src], c_("t1"))
                src = dst
            mark(vv.memset(tab_c[:, :, 0:1], 1.0))
            then(vv.memset(tab_s[:, :, 0:1], 0.0))
            tt = st.rearrange("p (q c) -> p q c", q=2 * Q)[:, 0:Q]
            n = 1
            while n < NC:
                k = (P, Q, n)
                cmul(tab_c[:, :, n:2 * n], tab_s[:, :, n:2 * n], (tab_c[:, :, 0:n], tab_s[:, :, 0:n]),
                     [z.unsqueeze(2).to_broadcast(k) for z in ph[src]], tt[:, :, 0:n])
                n *= 2
                if n < NC:
                    dst = 1 if src != 1 else 2
                    cmul(*ph[dst], ph[src], ph[src], c_("t1"))
                    src = dst

            v.wait_ge(diff_ready, MW)
            for h in range(2):
                qs = slice(8 * h, 8 * h + 8)
                b_re = full(v, ("bu", h, 0)).rearrange("p (q c) -> p q c", q=8)
                b_im = full(v, ("bu", h, 1)).rearrange("p (q c) -> p q c", q=8)
                mark(mul(rot[0], b_re, tab_c[:, qs]))
                mark(mul(rot[1], b_im, tab_s[:, qs]))
                then(mul(rot[2], b_re, tab_s[:, qs]))
                vv.tensor_tensor(st_re[:, qs], rot[0], rot[1], ALU.add).then_inc(out_of(("bu", h, 0)), 1)
                taken(v, ("bu", h, 0))
                then(mul(rot[0], b_im, tab_c[:, qs]))
                vv.tensor_tensor(st_im[:, qs], rot[0], rot[2], ALU.subtract).then_inc(out_of(("bu", h, 1)), 1)
                taken(v, ("bu", h, 1))
            for q in range(Q):
                decay = c_("rho")[:, q:q + 1].to_broadcast((P, NC))
                for z in (st_re, st_im):
                    mark(vv.tensor_tensor_scan(z[:, q], decay, z[:, q], 0.0, ALU.mult, ALU.add))
            step.wait()
            for h in range(2):
                qs, c0 = slice(8 * h, 8 * h + 8), slice(0, NC - 1)
                r0, r1, r2 = (r[:, :, c0] for r in rot)
                mark(mul(r0, st_re[:, qs, c0], tab_c[:, qs, c0]))
                mark(mul(r1, st_im[:, qs, c0], tab_s[:, qs, c0]))
                then(mul(r2, st_re[:, qs, c0], tab_s[:, qs, c0]))
                then(sub(st_re[:, qs, 1:NC], r0, r1))
                then(mul(r0, st_im[:, qs, c0], tab_c[:, qs, c0]))
                then(add(st_im[:, qs, 1:NC], r2, r0))
            then(vv.memset(st_re[:, :, 0:1], 0.0))
            vv.memset(st_im[:, :, 0:1], 0.0).then_inc(st_ready, 1)

            v.wait_ge(consts_in, 16 * 12)
            v.wait_ge(yT_in, 16)
            for m in range(MW):
                vv.scalar_tensor_tensor(yT[:, m], C[:, m], cols[:, DSK + m:DSK + m + 1], yT[:, m], ALU.mult, ALU.add).then_inc(ych_ready, 1)

            for i in range(NT):
                taken(v, ("v", i))
                then(vv.bn_stats(stat[:, 44:50], V[:, i]))
                mark(vv.bn_aggr(mean_var[:, 2 * i:2 * i + 2], stat[:, 44:50]))
                step.wait()
            v.wait_ge(consts_in, 16 * 12)
            vv.tensor_copy(stat[:, 32:36], mean_var[:].rearrange("p (i two) -> p two i", two=2)[:, 1]).then_inc(var_ready, 1)
            v.wait_ge(vstd_ready, 1)
            then(vv.reciprocal(stat[:, 36:40], stat[:, 40:44]))
            for i in range(NT):
                then(vv.tensor_scalar(V[:, i], V[:, i], mean_var[:, 2 * i:2 * i + 1], stat[:, 36 + i:37 + i], ALU.subtract, ALU.mult))
                then(mul(V[:, i], V[:, i], lng))
                add(V[:, i], V[:, i], lnb).then_inc(vn_ready, 1)

            for m in range(MW):
                taken(v, ("gl", m))
            for m in range(MW):
                vv.tensor_tensor(C[:, m], C[:, m], yT[:, m], ALU.mult).then_inc(yc_ready, 1)
            v.wait_ge(h_hi_ready, 1)
            full(v, ("v", NT - 1))
            vv.tensor_tensor(h_lo[:], hT, h_hi[:], ALU.subtract).then_inc(h_lo_ready, 1)

            def lower(n, s):
                v.wait_ge(w_hi_ready, 2 * (2 * n + s) + 2)
                mark(vv.tensor_tensor(wg_lo[s][:], slot_k[n % 2][:, :, SW * s:SW * (s + 1)], wg_hi[s][:], ALU.subtract))
                vv.tensor_tensor(wb_lo[s][:], wb_slot[n % 2][:, :, SW * s:SW * (s + 1)], wb_hi[s][:], ALU.subtract).then_inc(w_lo_ready, 1)

            lower(0, 0)
            lower(0, 1)

            taken(v, ("u", MW - 1))
            for h in range(4):
                name = ("sg", h)
                vv.tensor_tensor(U[:, h], U[:, h], full(v, name), ALU.mult).then_inc(out_of(name), 1)

            muls = 0
            for n, (half, k_) in enumerate(GATE_STEPS):
                if half == 0:
                    v.wait_ge(y_hi_ready, k_ + 1)
                    vv.tensor_tensor(y_lo[k_][:], (A, U, C)[k_], y_hi[:], ALU.subtract).then_inc(y_lo_ready, 1)
                for m in range(MW):
                    i = n * MW + m
                    name = ("br", n, m)
                    taken(v, ("gt", n, m))
                    bank, dst = full(v, name), M[:, half * MW + m]
                    if k_ == 0:
                        vv.tensor_tensor(dst, sig[i % 2], bank, ALU.mult).then_inc(out_of(name), 1)
                    else:
                        vv.tensor_tensor(prod, sig[i % 2], bank, ALU.mult).then_inc(merge_mul, 1)
                        muls += 1
                        v.wait_ge(merge_mul, muls)
                        vv.tensor_tensor(dst, dst, prod, ALU.add).then_inc(out_of(name), 1)
                    taken(v, name)
                    vv.tensor_copy(stat[:, 61:62], stat[:, 28:29]).then_inc(merge_done, 1)
                    if m % 2 == 1 and n < 5:
                        lower(n + 1, m // 2)

            v.wait_ge(x_again, 16)

            def residual(i):
                for h in range(2):
                    name = ("o", i, h)
                    dst = x3[:, i, W * h:W * (h + 1)]
                    vv.tensor_tensor(dst, dst, full(v, name), ALU.add).then_inc(out_of(name), 1)

            def normed(i):
                v.wait_ge(std2_ready, i + 1)
                then(vv.reciprocal(stat[:, 50 + i:51 + i], stat[:, 12 + i:13 + i]))
                if i >= 2:
                    v.wait_ge(h2_stored[i % 2], 16)
                    full(v, ("rt", i - 2, 1))
                vv.tensor_scalar(h2n[i % 2], x3[:, i], stat[:, 50 + i:51 + i], None, ALU.mult).then_inc(h2_ready, 1)

            def routed(i):
                for h in range(2):
                    name = ("rt", i, h)
                    vv.tensor_tensor(h2T[:, 4 * h:4 * h + 4], full(v, name).rearrange("p (k t) -> p k t", k=4),
                                     cols[:, GFF + 4 * h:GFF + 4 * h + 4].unsqueeze(2).to_broadcast((P, 4, P)),
                                     ALU.mult).then_inc(out_of(name), 1)
                name = ("lg", i)
                vv.tensor_copy(logits_zone[:, i], full(v, name)[:, 0:36]).then_inc(out_of(name), 1)

            for i in range(NT):
                residual(i)
                if i >= 1:
                    routed(i - 1)
                normed(i)
            routed(NT - 1)
            for i in range(NT):
                taken(v, ("lg", i))

            L4 = logits_zone[:, :, 0:4]
            L32 = logits_zone[:, :, 4:36].rearrange("p i (g e) -> p i g e", g=4)

            def first_max(vals, best, cand, low, onehot, width):
                sh = (P, NT, width)
                then(vv.tensor_reduce(best, vals, X, ALU.max))
                then(vv.tensor_tensor(onehot, vals, best.to_broadcast(sh), ALU.is_equal))
                then(vv.scalar_tensor_tensor(cand, onehot, -100.0, iot[:, 0:width].unsqueeze(1).to_broadcast(sh), ALU.mult, ALU.add))
                then(vv.tensor_reduce(low, cand, X, ALU.min))
                then(vv.tensor_tensor(onehot, cand, low.to_broadcast(sh), ALU.is_equal))

            first_max(L4, R["gmax"], R["cand"], R["cmin"], R["ohg"], 4)
            vv.tensor_tensor(R["dg"], L4, R["gmax"].to_broadcast((P, NT, 4)), ALU.subtract).then_inc(exp_in, 1)
            s4 = (P, NT, 4, GE)
            then(mul(R["sel"], L32, R["ohg"].unsqueeze(3).to_broadcast(s4)))
            then(vv.tensor_reduce(R["esel"], R["sel"].rearrange("p i g e -> p i e g"), X, ALU.add))
            first_max(R["esel"], R["m1"], R["cand8"], R["min8"], R["oh1"], GE)
            then(axpy(R["e2"], R["oh1"], -BIG, R["esel"]))
            first_max(R["e2"], R["m2"], R["cand8"], R["min8"], R["oh2"], GE)
            vv.tensor_tensor(R["dm"], R["m2"], R["m1"], ALU.subtract).then_inc(exp2_in, 1)
            for M_, o_ in (("M1", "oh1"), ("M2", "oh2")):
                mark(mul(R[M_], R["ohg"].unsqueeze(3).to_broadcast(s4), R[o_].unsqueeze(2).to_broadcast(s4)))
            step.wait()
            M1, M2 = (R[m].rearrange("p i g e -> p i (g e)") for m in ("M1", "M2"))
            add(oh, M1, M2).then_inc(onehot_ready, 1)
            v.wait_ge(exp_out, 1)
            then(vv.tensor_reduce(R["gsum"], R["ex4"], X, ALU.add))
            then(vv.reciprocal(R["gp"], R["gsum"]))
            v.wait_ge(exp2_out, 1)
            then(vv.tensor_scalar(R["den"], R["ex"], 1.0, None, ALU.add))
            then(vv.reciprocal(R["den"], R["den"]))
            w1, w2 = (wts[:, NT * c:NT * (c + 1)].unsqueeze(2) for c in range(2))
            then(mul(w1, R["den"], R["gp"]))
            then(mul(w2, w1, R["ex"]))
            mark(vv.tensor_scalar(R["e64"], iot[:, 0:NE], float(CAP), None, ALU.mult))
            bank = full(v, "pos")
            then(vv.tensor_copy(R["cnt"], bank[:, NE * NT:NE * (NT + 1)]))
            then(vv.tensor_scalar(R["has2"], R["cnt"], float(CAP), None, ALU.is_gt))
            then(vv.tensor_tensor_scan(R["cum2"], lnb[:, 0:NE], R["has2"], 0.0, ALU.mult, ALU.add))
            then(sub(R["ord2"], R["cum2"], R["has2"]))
            mark(vv.tensor_copy(second[0:1, 0], R["has2"][0:1]))
            mark(vv.tensor_copy(second[0:1, 1], R["ord2"][0:1]))
            then(vv.tensor_scalar(R["ov"], R["cnt"], float(2 * CAP), None, ALU.is_gt))
            for k in range(3, T // CAP):
                then(vv.scalar_tensor_tensor(R["ov"], R["cnt"], float(CAP * k), R["ov"], ALU.is_gt, ALU.add))
            then(vv.tensor_tensor_scan(R["incl"], lnb[:, 0:NE], R["ov"], 0.0, ALU.mult, ALU.add))
            then(sub(R["base"], R["incl"], R["ov"]))
            then(axpy(R["base"], R["base"], float(CAP), R["e64"], ALU.subtract))
            then(vv.tensor_scalar(R["base"], R["base"], float(NE * CAP - CAP), None, ALU.add))
            se = (P, NT, NE)
            vv.tensor_copy(R["pos"], bank[:, 0:NE * NT].rearrange("p (i e) -> p i e", i=NT)).then_inc(out_of("pos"), 1)
            taken(v, "pos")
            mark(vv.tensor_scalar(R["pick"], R["pos"], float(CAP), float(NE * CAP - CAP), ALU.is_ge, ALU.mult))
            then(vv.tensor_scalar(R["row"], R["pos"], float(2 * CAP), None, ALU.is_ge))
            then(mul(R["row"], R["row"], R["base"].unsqueeze(1).to_broadcast(se)))
            then(add(R["row"], R["row"], R["pick"]))
            then(add(R["row"], R["row"], R["pos"]))
            then(add(R["row"], R["row"], R["e64"].unsqueeze(1).to_broadcast(se)))
            for c, m in enumerate((M1, M2)):
                then(mul(R["pick"], R["row"], m))
                then(vv.tensor_reduce(R["rowf"][:, c:c + 1].rearrange("p a i -> p i a"), R["pick"], X, ALU.add))
            vv.tensor_copy(row_u[:], R["rowf"].rearrange("p c i -> p (c i)")).then_inc(rows_ready, 1)
            so = (1, NOV, NE)
            then(vv.tensor_tensor(R["le"][0:1], R["incl"][0:1].unsqueeze(1).to_broadcast(so),
                                  iot[0:1, 0:NOV].unsqueeze(2).to_broadcast(so), ALU.is_le))
            then(vv.tensor_reduce(R["eid"][0:1].unsqueeze(2), R["le"][0:1], X, ALU.add))
            then(vv.tensor_scalar(ovi[0:1, 0:NOV], R["eid"][0:1], float(NE - 1), None, ALU.min))
            vv.tensor_copy(ovi[0:1, NOV:NOV + 1], R["incl"][0:1, NE - 1:NE]).then_inc(ov_ready, 1)
            vv.tensor_copy(idx_u[:], full(v, "tok")[0:CAP, 0:NB]).then_inc(out_of("tok"), 1)
            taken(v, "tok")
            vv.tensor_copy(stat[:, 61:62], stat[:, 28:29]).then_inc(idx_ready, 1)
            experts_vector(v)

        @block.gpsimd
        def _(gp):
            g = nc.gpsimd
            step = Steps(gp, gp_step)
            then, mark = step.then, step.mark
            then(g.memset(ident[:], 0.0))
            g.affine_select(out=ident[:], in_=ident[:], compare_op=ALU.not_equal, fill=1.0, base=0,
                            pattern=[[-1, P]], channel_multiplier=1).then_inc(ident_ready, 1)
            gp.wait_ge(params_in, 16 * 8)
            g.tensor_copy(par_nat[:, 2].rearrange("q (two p) -> q two p", two=2),
                          ldt_nat.unsqueeze(2).to_broadcast((Q, 2, S))).then_inc(ldt_spread, 1)
            g.affine_select(out=sgw_nat, in_=sgw_nat, compare_op=ALU.is_ge, fill=0.0, base=0,
                            pattern=[[0, 4], [-1, P]], channel_multiplier=1).then_inc(sgw_masked, 1)
            mark(g.memset(ones_row[:], 1.0))
            for i in range(16):
                mark(g.memset(icnt[:, i:i + 1], 1.0 / (i + 1)))
            mark(g.iota(iot_i[:, 0:48], pattern=[[1, 48]], base=0, channel_multiplier=0))
            then(g.iota(iot_i[:, 48:52], pattern=[[P, NT]], base=0, channel_multiplier=1))
            then(g.tensor_copy(iot[:], iot_i[:]))
            for w_ in win:
                mark(g.memset(w_[:, 0:PAD], 0.0))
            then(g.memset(zeros[:], 0.0))
            g.memset(eps, EPS).then_inc(consts_made, 1)
            gp.dma_start(tok_d.rearrange("(n c) a -> n (c a)", n=NB), zeros[:]).then_inc(tok_zero, 16)
            full(gp, ("x", NT - 1, 1))
            g.memset(xb[:], 0.0).then_inc(toep_zero, 1)
            for m in range(MW):
                taken(gp, ("a", m))
                src, wide = A[:, m], 2 ** (m + 1)
                cur = 0
                then(g.tensor_copy(win[0][:, PAD:], src))
                for k in range(m + 1):
                    s_ = 2 ** k
                    then(g.tensor_tensor(win[1 - cur][:, PAD:], win[cur][:, PAD:], win[cur][:, PAD - s_:PAD + T - s_], ALU.add))
                    cur = 1 - cur
                w_ = win[cur]
                mark(g.tensor_tensor(w_[:, PAD:PAD + wide], w_[:, PAD:PAD + wide], icnt[:, 0:wide], ALU.mult))
                then(g.tensor_scalar(w_[:, PAD + wide:], w_[:, PAD + wide:], 1.0 / wide, None, ALU.mult))
                g.tensor_tensor(src, w_[:, PAD:], src, ALU.subtract).then_inc(diff_ready, 1)
                gp.wait_ge(diff_ready, m + 1)
            full(gp, ("br", 5, MW - 1))
            mark(g.memset(lnb[:, 0:P], 1.0))
            then(g.memset(lng[:, 0:P], 1.0))
            g.affine_select(out=lng[:, 0:P], in_=lng[:, 0:P], compare_op=ALU.is_gt, fill=0.0, base=0,
                            pattern=[[1, P]], channel_multiplier=-1).then_inc(masks_ready, 1)
            for i in range(NT):
                gp.wait_ge(h2_ready, i + 1)
                gp.dma_start(h2_d[i * P:(i + 1) * P, :], h2n[i % 2]).then_inc(h2_stored[i % 2], 16)
            gp.wait_ge(tok_zero, 16)
            gp.wait_ge(rows_ready, 1)
            for c in range(2):
                for i in range(NT):
                    j = NT * c + i
                    g.indirect_dma_start(tok_d, bass.IndirectOffsetOnAxis(ap=row_u[:, j:j + 1], axis=0),
                                         iot[:, 48 + i:49 + i], None).then_inc(tok_scattered, 16)
            gp.wait_ge(tok_scattered, 16 * 2 * NT)
            gp.dma_start(tok_rows, tok_d.rearrange("(n c) a -> n (c a)", n=NB)).then_inc(tok_in, 16)
            experts_gpsimd(gp)


INPUTS = ["x", "norm_mix_g", "w_in", "b_gate", "pool_w", "pool_scale", "sgu_ln_g", "sgu_ln_b", "sgu_w", "sgu_b",
          "ssm_a_re", "ssm_a_im", "ssm_log_dt", "ssm_b_re", "ssm_b_im", "ssm_c_re", "ssm_c_im", "ssm_d", "glu_w",
          "glu_b", "w_branch", "w_out", "norm_ffn_g", "router_group_w", "router_group_b", "router_expert_w",
          "router_expert_b", "exp_w_gate", "exp_w_up", "exp_w_down", "norm_final_g"]


def kernel(**inputs):
    import concourse.bacc as bacc
    from concourse.bass_utils import run_bass_kernel_spmd

    nc = bacc.Bacc("TRN2", target_bir_lowering=False, num_devices=1)
    arrays, args = {}, []
    for name in INPUTS:
        a = np.ascontiguousarray(inputs[name])
        arrays[f"in_{name}"] = a
        args.append(nc.dram_tensor(f"in_{name}", a.shape, mybir.dt.from_np(a.dtype), kind="ExternalInput").ap())
    args.append(nc.dram_tensor("out", (1, T, D), F32, kind="ExternalOutput").ap())
    trunk(nc, *args)
    r = run_bass_kernel_spmd(nc, [arrays], core_ids=[0])
    return r.results[0]["out"]
```
